# Optimizing a Trainium2 kernel written in Bass

```python
import jax, jax.numpy as jnp
from jax import lax
import numpy as np

D_MODEL = 1024
BATCH = 1
SEQ = 256
DEPTH = 2

CHUNK = 64
N_EVEN = (DEPTH + 1) // 2
N_ODD = DEPTH // 2

D_POOL = D_MODEL // 2
N_POOL_GROUPS = 4
POOL_WINDOWS = (2, 4, 8, 16)
D_POOL_GROUP = D_POOL // N_POOL_GROUPS
D_CONV = D_MODEL - D_POOL
CONV_WIDTH = 31
D_EVEN_IN = D_POOL + 2 * D_CONV

HEAD_DIM = 64
D_ATTN = D_MODEL // 2
N_ATTN_HEADS = D_ATTN // HEAD_DIM
D_SC = D_MODEL - D_ATTN
SC_WIDTH = 3
Q_BLOCK = 128
D_ODD_IN = 3 * D_ATTN + N_ATTN_HEADS + 3 * D_SC

D_FF = 2816
N_EXPERTS = 8
TOP_K = 2
D_EXPERT = 3584
NORM_EPS = 1e-6

kernel_name = "hybrid_pool_conformer_fox_shortconv_moe"

def rmsnorm(x, g):
    xf = x.astype(jnp.float32)
    y = xf * lax.rsqrt(jnp.mean(xf * xf, axis=-1, keepdims=True) + NORM_EPS)
    return (y * g.astype(jnp.float32)).astype(x.dtype)

def layernorm(x, g, b):
    xf = x.astype(jnp.float32)
    mu = jnp.mean(xf, axis=-1, keepdims=True)
    xc = xf - mu
    y = xc * lax.rsqrt(jnp.mean(xc * xc, axis=-1, keepdims=True) + NORM_EPS)
    return (y * g.astype(jnp.float32) + b.astype(jnp.float32)).astype(x.dtype)

def causal_depthwise_conv(x, w):
    K, C = w.shape
    return lax.conv_general_dilated(
        x, w[:, None, :].astype(x.dtype), window_strides=(1,),
        padding=[(K - 1, 0)], dimension_numbers=("NWC", "WIO", "NWC"),
        feature_group_count=C)

def multiscale_pool(xa, w_group, scale):
    Bn, S, C = xa.shape
    xf = xa.astype(jnp.float32)
    csum = jnp.pad(jnp.cumsum(xf, axis=1), ((0, 0), (1, 0), (0, 0)))
    win = jnp.repeat(jnp.array(POOL_WINDOWS, jnp.int32), D_POOL_GROUP)
    t = jnp.arange(S, dtype=jnp.int32)[:, None]
    start = jnp.maximum(t - win[None, :] + 1, 0)
    lagged = jnp.take_along_axis(csum, jnp.broadcast_to(start[None], (Bn, S, C)), axis=1)
    count = (t - start + 1).astype(jnp.float32)
    pooled = ((csum[:, 1:] - lagged) / count - xf).astype(xa.dtype)
    pooled = pooled.reshape(Bn, S, N_POOL_GROUPS, D_POOL_GROUP)
    y = jnp.einsum("bsgc,gcd->bsgd", pooled, w_group).reshape(Bn, S, C)
    return y * scale

def conformer_conv(val, gate, dw_w, dw_b, ln_g, ln_b):
    u = val * jax.nn.sigmoid(gate)
    u = causal_depthwise_conv(u, dw_w) + dw_b
    u = layernorm(u, ln_g, ln_b)
    return jax.nn.silu(u)

def forgetting_attention(q, k, v, log_f):
    S = q.shape[2]
    F = jnp.cumsum(log_f, axis=-1)
    scale = HEAD_DIM ** -0.5
    outs = []
    for blk in range(S // Q_BLOCK):
        q0, q1 = blk * Q_BLOCK, (blk + 1) * Q_BLOCK
        s = jnp.einsum("bhqd,bhkd->bhqk", q[:, :, q0:q1], k[:, :, :q1]).astype(jnp.float32) * scale
        s = s + F[:, :, q0:q1, None] - F[:, :, None, :q1]
        mask = jnp.arange(q0, q1)[:, None] >= jnp.arange(q1)[None, :]
        p = jax.nn.softmax(jnp.where(mask, s, -jnp.inf), axis=-1)
        outs.append(jnp.einsum("bhqk,bhkd->bhqd", p.astype(v.dtype), v[:, :, :q1]))
    return jnp.concatenate(outs, axis=2)

def swiglu(h, w_gate, w_up, w_down):
    return (jax.nn.silu(h @ w_gate) * (h @ w_up)) @ w_down

def moe_swiglu(h, router_w, router_b, w_gate, w_up, w_down):
    Bn, S, D = h.shape
    ht = h.reshape(Bn * S, D)
    logits = (ht @ router_w).astype(jnp.float32) + router_b.astype(jnp.float32)
    top_val, top_idx = lax.top_k(logits, TOP_K)
    gates = jax.nn.softmax(top_val, axis=-1)
    combine = jnp.sum(jax.nn.one_hot(top_idx, N_EXPERTS, dtype=jnp.float32) * gates[..., None], axis=1)
    combine = combine.astype(h.dtype)
    out = jnp.zeros_like(ht)
    for e in range(N_EXPERTS):
        out = out + combine[:, e:e + 1] * swiglu(ht, w_gate[e], w_up[e], w_down[e])
    return out.reshape(Bn, S, D)

def setup_inputs(seed: int = 0) -> dict:
    key = jax.random.key(seed)
    ks = iter(jax.random.split(key, 32))

    def nrm(shape, scale):
        return jax.random.normal(next(ks), shape, jnp.float32) * scale

    def gain(shape):
        return 1.0 + nrm(shape, 0.05)

    E, O = N_EVEN, N_ODD
    head_offsets = jnp.linspace(1.0, 4.0, N_ATTN_HEADS, dtype=jnp.float32)
    return {
        "x": nrm((BATCH, SEQ, D_MODEL), 1.0),
        "ev_norm_mix": gain((E, D_MODEL)),
        "ev_w_in": nrm((E, D_MODEL, D_EVEN_IN), D_MODEL ** -0.5),
        "pool_w": nrm((E, N_POOL_GROUPS, D_POOL_GROUP, D_POOL_GROUP), D_POOL_GROUP ** -0.5),
        "pool_scale": gain((E, D_POOL)),
        "conv_dw_w": nrm((E, CONV_WIDTH, D_CONV), CONV_WIDTH ** -0.5),
        "conv_dw_b": nrm((E, D_CONV), 0.02),
        "conv_ln_g": gain((E, D_CONV)),
        "conv_ln_b": nrm((E, D_CONV), 0.02),
        "ev_w_out": nrm((E, D_POOL + D_CONV, D_MODEL), (D_POOL + D_CONV) ** -0.5),
        "ev_norm_ffn": gain((E, D_MODEL)),
        "ffn_w_gate": nrm((E, D_MODEL, D_FF), D_MODEL ** -0.5),
        "ffn_w_up": nrm((E, D_MODEL, D_FF), D_MODEL ** -0.5),
        "ffn_w_down": nrm((E, D_FF, D_MODEL), D_FF ** -0.5),
        "od_norm_mix": gain((O, D_MODEL)),
        "od_w_in": nrm((O, D_MODEL, D_ODD_IN), D_MODEL ** -0.5),
        "forget_bias": head_offsets[None, :] + nrm((O, N_ATTN_HEADS), 0.1),
        "q_norm_g": gain((O, HEAD_DIM)),
        "k_norm_g": gain((O, HEAD_DIM)),
        "sc_conv_w": nrm((O, SC_WIDTH, D_SC), SC_WIDTH ** -0.5),
        "od_w_out": nrm((O, D_ATTN + D_SC, D_MODEL), (D_ATTN + D_SC) ** -0.5),
        "od_norm_ffn": gain((O, D_MODEL)),
        "router_w": nrm((O, D_MODEL, N_EXPERTS), D_MODEL ** -0.5),
        "router_b": nrm((O, N_EXPERTS), 0.01),
        "moe_w_gate": nrm((O, N_EXPERTS, D_MODEL, D_EXPERT), D_MODEL ** -0.5),
        "moe_w_up": nrm((O, N_EXPERTS, D_MODEL, D_EXPERT), D_MODEL ** -0.5),
        "moe_w_down": nrm((O, N_EXPERTS, D_EXPERT, D_MODEL), D_EXPERT ** -0.5),
    }

def reference(x, ev_norm_mix, ev_w_in, pool_w, pool_scale, conv_dw_w, conv_dw_b,
              conv_ln_g, conv_ln_b, ev_w_out, ev_norm_ffn, ffn_w_gate, ffn_w_up,
              ffn_w_down, od_norm_mix, od_w_in, forget_bias, q_norm_g, k_norm_g,
              sc_conv_w, od_w_out, od_norm_ffn, router_w, router_b, moe_w_gate,
              moe_w_up, moe_w_down):
    Bn, S, D = x.shape
    for layer in range(DEPTH):
        i = layer // 2
        if layer % 2 == 0:
            h = rmsnorm(x, ev_norm_mix[i])
            proj = h @ ev_w_in[i]
            xa = proj[..., :D_POOL]
            val = proj[..., D_POOL:D_POOL + D_CONV]
            gate = proj[..., D_POOL + D_CONV:]
            ya = multiscale_pool(xa, pool_w[i], pool_scale[i])
            yb = conformer_conv(val, gate, conv_dw_w[i], conv_dw_b[i], conv_ln_g[i], conv_ln_b[i])
            x = x + jnp.concatenate([ya, yb], axis=-1) @ ev_w_out[i]
            x = x + swiglu(rmsnorm(x, ev_norm_ffn[i]), ffn_w_gate[i], ffn_w_up[i], ffn_w_down[i])
        else:
            h = rmsnorm(x, od_norm_mix[i])
            proj = h @ od_w_in[i]
            o = 0
            q = proj[..., o:o + D_ATTN]; o += D_ATTN
            k = proj[..., o:o + D_ATTN]; o += D_ATTN
            v = proj[..., o:o + D_ATTN]; o += D_ATTN
            f_logit = proj[..., o:o + N_ATTN_HEADS]; o += N_ATTN_HEADS
            sx = proj[..., o:o + D_SC]; o += D_SC
            sb = proj[..., o:o + D_SC]; o += D_SC
            sc = proj[..., o:o + D_SC]

            def heads(t):
                return t.reshape(Bn, S, N_ATTN_HEADS, HEAD_DIM).transpose(0, 2, 1, 3)

            qh = rmsnorm(heads(q), q_norm_g[i])
            kh = rmsnorm(heads(k), k_norm_g[i])
            vh = heads(v)
            log_f = jax.nn.log_sigmoid(f_logit.astype(jnp.float32)
                                       + forget_bias[i].astype(jnp.float32)).transpose(0, 2, 1)
            yc = forgetting_attention(qh, kh, vh, log_f).transpose(0, 2, 1, 3).reshape(Bn, S, D_ATTN)
            yd = sb * causal_depthwise_conv(sc * sx, sc_conv_w[i])
            x = x + jnp.concatenate([yc, yd], axis=-1) @ od_w_out[i]
            x = x + moe_swiglu(rmsnorm(x, od_norm_ffn[i]), router_w[i], router_b[i],
                               moe_w_gate[i], moe_w_up[i], moe_w_down[i])
    return x


_drawn_inputs = setup_inputs


def setup_inputs(seed=0):
    import zlib

    import numpy as np

    out = dict(_drawn_inputs(seed))
    spreads = {}
    factors = {'conv_ln_b': 3.723, 'q_norm_g': 4.146, 'k_norm_g': 4.582, 'router_b': 3.09}
    for name, (base, spread) in spreads.items():
        noise = np.random.default_rng([zlib.crc32(name.encode()), seed]).standard_normal(out[name].shape)
        drawn = base * np.exp(spread * noise) if base else spread * noise
        out[name] = __import__('jax').numpy.asarray(drawn.astype(out[name].dtype))
    for name, factor in factors.items():
        out[name] = (out[name] * factor).astype(out[name].dtype)
    return out
```

```python
from contextlib import ExitStack

import concourse.bass as bass
from concourse import mybir

F32 = mybir.dt.float32
I32 = mybir.dt.int32
ALU = mybir.AluOpType
ACT = mybir.ActivationFunctionType
AX = mybir.AxisListType

P = 128
UNIT = 2048
RING = 7
EPS = 1e-6
WINDOWS = (2, 4, 8, 16)
NEG = -1.0e30


def build_trunk(nc, a, out):
    T, D = a["x"].shape[1:]
    TT, DT = T // P, D // P
    C = a["pool_scale"].shape[1]
    CT = C // P
    TAPS = a["conv_dw_w"].shape[1]
    STAPS = a["sc_conv_w"].shape[1]
    F = a["ffn_w_gate"].shape[2]
    NH = a["forget_bias"].shape[1]
    HD = a["q_norm_g"].shape[1]
    NE = a["router_w"].shape[2]
    FE = a["moe_w_gate"].shape[3]
    PADC, PADS, PADP = TAPS - 1, STAPS - 1, max(WINDOWS) - 1
    FB = F // 256
    EB = FE // 512

    def cols_unit(w, c0):
        return w[:, c0:c0 + 256].rearrange("(k p) n -> p k n", p=P), DT, 256

    def half_unit(w, k0, c0):
        return w[k0 * P:(k0 + 4) * P, c0:c0 + 512].rearrange("(k p) n -> p k n", p=P), 4, 512

    def rows_unit(w, k0):
        return w[k0 * P:(k0 + 2) * P, :].rearrange("(k p) n -> p k n", p=P), 2, D

    ev_in, od_in = a["ev_w_in"][0], a["od_w_in"][0]
    wg, wu, wd = a["ffn_w_gate"][0], a["ffn_w_up"][0], a["ffn_w_down"][0]
    units = [cols_unit(ev_in, c) for c in (C, 2 * C, C + 256, 2 * C + 256, 0, 256)]
    E_IN = 0
    E_OUT = len(units)
    units += [rows_unit(a["ev_w_out"][0], 2 * m) for m in range(DT // 2)]
    FFN = len(units)
    ffn_gate, ffn_up, ffn_down = {}, {}, {}
    for j in range(FB + 1):
        if j < FB:
            ffn_gate[j] = len(units)
            units.append(cols_unit(wg, 256 * j))
            ffn_up[j] = len(units)
            units.append(cols_unit(wu, 256 * j))
        if j >= 1:
            ffn_down[j - 1] = len(units)
            units.append(rows_unit(wd, 2 * (j - 1)))
    O_IN = len(units)
    S0 = 3 * C + NH
    units += [cols_unit(od_in, c) for c in (0, 256, C, C + 256)]
    units += [half_unit(od_in, k, 2 * C) for k in (0, 4)]
    units += [cols_unit(od_in, S0 + c) for c in (0, 256, 2 * C, 2 * C + 256, C, C + 256)]
    O_Q, O_K, O_V, O_SX, O_SC, O_SB = O_IN, O_IN + 2, O_IN + 4, O_IN + 6, O_IN + 8, O_IN + 10
    O_OUT = len(units)
    units += [rows_unit(a["od_w_out"][0], 2 * m) for m in range(DT // 2)]
    MOE = len(units)
    moe_gate, moe_up, moe_down, PER = {}, {}, {}, 0
    expert_units = []
    for c in range(EB + 1):
        if c < EB:
            moe_gate[c], moe_up[c] = PER, PER + 2
            expert_units += [("moe_w_gate", 4 * h, 512 * c) for h in (0, 1)]
            expert_units += [("moe_w_up", 4 * h, 512 * c) for h in (0, 1)]
            PER += 4
        if c >= 1:
            moe_down[c - 1] = PER
            expert_units += [("moe_w_down", 4 * (c - 1) + 2 * h, None) for h in (0, 1)]
            PER += 2
    assert PER == len(expert_units) and PER % RING == 0

    with ExitStack() as ctx:
        def sb(name, shape, dt=F32):
            return ctx.enter_context(nc.sbuf_tensor(name, shape, dt))

        def sem(name):
            return ctx.enter_context(nc.semaphore(name))

        ring = sb("ring", [P, RING, UNIT])
        resid = sb("resid", [P, TT, D])
        normed = sb("normed", [P, TT, D])
        hT = sb("hT", [P, DT, T])
        mixT = sb("mixT", [P, DT, T])
        wide = sb("wide", [P, 2, 512])
        hid = sb("hid", [P, 2, 2, T])
        upad = sb("upad", [P, CT, PADC + T])
        cacc = sb("cacc", [P, CT, T])
        xpad = sb("xpad", [P, CT, PADP + T])
        winA = sb("winA", [P, CT, PADP + T])
        winB = sb("winB", [P, CT, PADP + T])
        rcount = sb("rcount", [P, CT, T])
        poolw = sb("poolw", [P, CT, P])
        ss = sb("ss", [P, 4, TT])
        rstd = sb("rstd", [P, 4, TT])
        vrow = sb("vrow", [P, P])
        drow = sb("drow", [P, P])
        vcol = sb("vcol", [P, P])
        dcol = sb("dcol", [P, P])
        ident = sb("ident", [P, P])
        ones = sb("ones", [P, T])
        headmean = sb("headmean", [P, P])
        lnmean = sb("lnmean", [P, P])
        before = sb("before", [P, P])
        causal = sb("causal", [P, P])
        sel = sb("sel", [NH, NH, T])
        eps = sb("eps", [P, 1])
        iota = sb("iota", [P, T])
        qkg = sb("qkg", [P, 2])
        fb = sb("fb", [NH, 1])
        wf = sb("wf", [P, DT, NH])
        wr = sb("wr", [P, DT, NE])
        rb = sb("rb", [P, NE])
        qkT = sb("qkT", [P, 4, 2, T])
        qsq = sb("qsq", [P, 4, 512])
        v = sb("v", [P, TT, C])
        fl = sb("fl", [NH, 6, T])
        probs = sb("probs", [P, 2, T])
        probsT = sb("probsT", [P, 2, T])
        rmax = sb("rmax", [P, 2 * NH, 4])
        sxs = sb("sxs", [P, CT, T])
        spad = sb("spad", [P, CT, PADS + T])
        sacc = sb("sacc", [P, CT, T])
        lg = sb("lg", [P, TT, 12, NE])
        idx = sb("idx", [P, TT, 8], mybir.dt.uint32)
        pos = sb("pos", [P, 2, TT, NE])
        comb = sb("comb", [P, TT, NE])
        cnt = sb("cnt", [P, 2])
        over = sb("over", [P, 1], I32)
        disp = sb("disp", [P, TT, P])
        dispw = sb("dispw", [P, TT, P])
        dispT = sb("dispT", [P, TT, P])
        xe = sb("xe", [P, DT, P])
        act = sb("act", [P, 2, 512])
        ehid = sb("ehid", [P, 2, 512])
        ehidT = sb("ehidT", [P, 2, 4, P])
        ye = sb("ye", [P, D])

        bank = [ctx.enter_context(nc.psum_tensor(f"bank{i}", [P, 512], F32)) for i in range(8)]

        loaded = [sem(f"loaded{s}") for s in range(RING)]
        unit_done = sem("unit_done")
        vectors_loaded = sem("vectors_loaded")
        small_loaded = sem("small_loaded")
        x_loaded = sem("x_loaded")
        pool_const = sem("pool_const")
        consts = sem("consts")
        dve_const = sem("dve_const")
        vec_turned = sem("vec_turned")
        vec_ready = sem("vec_ready")
        sq_done = sem("sq_done")
        rms_ready = sem("rms_ready")
        rstd_ready = sem("rstd_ready")
        normed_ready = sem("normed_ready")
        turned = sem("turned")
        hT_lo = sem("hT_lo")
        hT_hi = sem("hT_hi")
        sig_ready = sem("sig_ready")
        u_ready = sem("u_ready")
        xpad_ready = sem("xpad_ready")
        pool_step = sem("pool_step")
        pooled_ready = sem("pooled_ready")
        poolmix_done = sem("poolmix_done")
        poolT_ready = sem("poolT_ready")
        conv_step = sem("conv_step")
        conv_ready = sem("conv_ready")
        mean_done = sem("mean_done")
        xc_ready = sem("xc_ready")
        csq_ready = sem("csq_ready")
        cvar_done = sem("cvar_done")
        crms_ready = sem("crms_ready")
        crstd_ready = sem("crstd_ready")
        cn_ready = sem("cn_ready")
        convT_ready = sem("convT_ready")
        resid_ready = sem("resid_ready")
        silu_ready = sem("silu_ready")
        hid_ready = sem("hid_ready")
        f_done = sem("f_done")
        f_step = sem("f_step")
        f_act = sem("f_act")
        f_ready = sem("f_ready")
        qsq_ready = sem("qsq_ready")
        qms_done = sem("qms_done")
        qrms_ready = sem("qrms_ready")
        qrstd_ready = sem("qrstd_ready")
        qk_ready = sem("qk_ready")
        v_ready = sem("v_ready")
        sx_copied = sem("sx_copied")
        s_step = sem("s_step")
        z_ready = sem("z_ready")
        shortT_ready = sem("shortT_ready")
        score_done = sem("score_done")
        max_step = sem("max_step")
        max_ready = sem("max_ready")
        exp_ready = sem("exp_ready")
        p_step = sem("p_step")
        p_ready = sem("p_ready")
        pT_done = sem("pT_done")
        pT_ready = sem("pT_ready")
        o_done = sem("o_done")
        o_copied = sem("o_copied")
        logits_done = sem("logits_done")
        r_step = sem("r_step")
        r_exp = sem("r_exp")
        mask_ready = sem("mask_ready")
        count_done = sem("count_done")
        route_ready = sem("route_ready")
        over_ready = sem("over_ready")
        disp_ready = sem("disp_ready")
        gathered = sem("gathered")
        xe_ready = sem("xe_ready")
        dispT_done = sem("dispT_done")
        dispT_ready = sem("dispT_ready")
        act_ready = sem("act_ready")
        ehid_ready = sem("ehid_ready")
        ehidT_done = sem("ehidT_done")
        ehidT_ready = sem("ehidT_ready")
        ye_ready = sem("ye_ready")
        scattered = sem("scattered")
        added = sem("added")
        out_ready = sem("out_ready")
        out_stored = sem("out_stored")

        rows, n = {}, 0
        for name, k in (("ev_norm_mix", DT), ("ev_norm_ffn", DT), ("od_norm_mix", DT), ("od_norm_ffn", DT),
                        ("pool_scale", CT), ("conv_dw_b", CT), ("conv_ln_g", CT), ("conv_ln_b", CT)):
            rows[name] = (n, k)
            n += k
        SCW = n
        NV = n + STAPS * CT
        ND = TAPS * CT

        def col(name, k):
            i = rows[name][0] + k
            return vcol[:, i:i + 1]

        norms = ("ev_norm_mix", "ev_norm_ffn", "od_norm_mix", "od_norm_ffn")
        VECTORS, SMALL = 16 * (len(rows) + 2), 16 * 9

        def slot(u):
            return u % RING, u // RING + 1

        def view(u, k, n_):
            return ring[:, u % RING, :].rearrange("p (k n) -> p k n", k=k)

        block = ctx.enter_context(nc.Block())

        def run(eng, expert, last):
            with eng.Fori(0, NE) as i:
                expert(i, i, 0)
            eng.wait_ge(over_ready, 1)
            more = eng.value_load(over[0:1, 0:1], min_val=0, max_val=1)
            with eng.If(more == 1):
                with eng.Fori(NE, 2 * NE) as i:
                    expert(i, i - NE, 1)
                last(2)
            with eng.Else():
                last(1)

        @block.sync
        def _(sp):
            sp.dma_start(resid[:, :, :], a["x"][0].rearrange("(t p) d -> p t d", p=P)).then_inc(x_loaded, 16)
            for name, (r, k) in rows.items():
                sp.dma_start(vrow[r:r + k, :], a[name][0].rearrange("(k p) -> k p", p=P)).then_inc(vectors_loaded, 16)
            sp.dma_start(vrow[SCW:NV, :], a["sc_conv_w"][0].rearrange("s (k p) -> (s k) p", p=P)).then_inc(vectors_loaded, 16)
            sp.dma_start(drow[0:ND, :], a["conv_dw_w"][0].rearrange("s (k p) -> (s k) p", p=P)).then_inc(vectors_loaded, 16)

            def load(u, src, k, n_):
                s, times = slot(u)
                if u >= RING:
                    sp.wait_ge(unit_done, u - RING + 1)
                sp.dma_start(view(u, k, n_), src).then_inc(loaded[s], 16)

            for u, (src, k, n_) in enumerate(units):
                load(u, src, k, n_)
                if u == 1:
                    for r in range(P // HD):
                        sp.dma_start(qkg[r * HD:(r + 1) * HD, 0:1], a["q_norm_g"].rearrange("a d -> d a")).then_inc(small_loaded, 16)
                        sp.dma_start(qkg[r * HD:(r + 1) * HD, 1:2], a["k_norm_g"].rearrange("a d -> d a")).then_inc(small_loaded, 16)
                    sp.dma_start(poolw[:, :, :], a["pool_w"][0].rearrange("g c d -> c g d")).then_inc(small_loaded, 16)
                    sp.dma_start(fb[:, :], a["forget_bias"].rearrange("a h -> h a")).then_inc(small_loaded, 16)
                    sp.dma_start(wf[:, :, :], od_in[:, 3 * C:3 * C + NH].rearrange("(k p) n -> p k n", p=P)).then_inc(small_loaded, 16)
                    sp.dma_start(wr[:, :, :], a["router_w"][0].rearrange("(k p) n -> p k n", p=P)).then_inc(small_loaded, 16)
                    sp.dma_start(rb[:, :], a["router_b"][0:1, :].to_broadcast([P, NE])).then_inc(small_loaded, 16)

            def load_experts(i, e):
                for j, (name, k0, c0) in enumerate(expert_units):
                    u = MOE + j
                    if c0 is None:
                        src = a[name][0][e, k0 * P:(k0 + 2) * P, :].rearrange("(k p) n -> p k n", p=P)
                        k, n_ = 2, D
                    else:
                        src = a[name][0][e, k0 * P:(k0 + 4) * P, c0:c0 + 512].rearrange("(k p) n -> p k n", p=P)
                        k, n_ = 4, 512
                    sp.wait_ge(unit_done, i * PER + (u - RING + 1))
                    sp.dma_start(view(u, k, n_), src).then_inc(loaded[u % RING], 16)

            run(sp, lambda i, e, group: load_experts(i, e), lambda times: sp.nop())
            sp.wait_ge(out_ready, 1)
            sp.dma_start(out[0].rearrange("(t p) d -> p t d", p=P), resid[:, :, :]).then_inc(out_stored, 16)
            sp.wait_ge(out_stored, 16)

        @block.gpsimd
        def _(pool):
            n = [0]

            def chain(ins):
                n[0] += 1
                ins.then_inc(pool_const, 1)
                pool.wait_ge(pool_const, n[0])

            chain(pool.memset(eps[:, :], EPS))
            pool.memset(xpad[:, :, :], 0.0).then_inc(consts, 1)
            pool.memset(upad[:, :, :], 0.0).then_inc(consts, 1)
            chain(pool.memset(ident[:, :], 0.0))
            chain(pool.affine_select(out=ident[:, :], in_=ident[:, :], compare_op=ALU.not_equal, fill=1.0, base=0,
                                     pattern=[[-1, P]], channel_multiplier=1))
            pool.memset(ones[:, :], 1.0).then_inc(consts, 1)
            pool.memset(lnmean[:, :], 1.0 / C).then_inc(consts, 1)
            pool.memset(spad[:, :, :], 0.0).then_inc(consts, 1)
            chain(pool.iota(iota[:, :], pattern=[[1, T]], base=0, channel_multiplier=0,
                            allow_small_or_imprecise_dtypes=True))

            chain(pool.memset(before[:, :], 1.0))
            chain(pool.affine_select(out=before[:, :], in_=before[:, :], compare_op=ALU.is_gt, fill=0.0, base=0,
                                     pattern=[[1, P]], channel_multiplier=-1))
            chain(pool.memset(causal[:, :], 0.0))
            chain(pool.affine_select(out=causal[:, :], in_=causal[:, :], compare_op=ALU.is_ge, fill=NEG, base=0,
                                     pattern=[[-1, P]], channel_multiplier=1))
            chain(pool.memset(sel[:, :, :], 0.0))
            chain(pool.affine_select(out=sel[:, :, :], in_=sel[:, :, :], compare_op=ALU.not_equal, fill=1.0, base=0,
                                     pattern=[[-1, NH], [0, T]], channel_multiplier=1))
            pool.memset(headmean[:, :], 0.0).then_inc(pool_const, 1)
            n[0] += 1
            pool.wait_ge(pool_const, n[0])
            for r in range(P // HD):
                pool.memset(headmean[r * HD:(r + 1) * HD, r * HD:(r + 1) * HD], 1.0 / HD).then_inc(consts, 1)
                pool.wait_ge(consts, 6 + r)

            m = [0]

            def step(ins):
                m[0] += 1
                ins.then_inc(pool_step, 1)
                pool.wait_ge(pool_step, m[0])

            L = PADP + T
            pool.wait_ge(xpad_ready, 2)
            step(pool.tensor_tensor(winA[:, :, 1:L], xpad[:, :, 1:L], xpad[:, :, 0:L - 1], ALU.add))
            step(pool.tensor_tensor(winB[:, 1:, 3:L], winA[:, 1:, 3:L], winA[:, 1:, 1:L - 2], ALU.add))
            step(pool.tensor_tensor(winA[:, 2:, 7:L], winB[:, 2:, 7:L], winB[:, 2:, 3:L - 4], ALU.add))
            step(pool.tensor_tensor(winB[:, 3, 15:L], winA[:, 3, 15:L], winA[:, 3, 7:L - 8], ALU.add))
            pool.wait_ge(dve_const, 2 * CT)
            for g in range(CT):
                w = (winA if g % 2 == 0 else winB)[:, g, PADP:L]
                step(pool.tensor_tensor(w, w, rcount[:, g, :], ALU.mult))
            for g in range(CT):
                w = (winA if g % 2 == 0 else winB)[:, g, PADP:L]
                pool.tensor_tensor(w, w, xpad[:, g, PADP:L], ALU.subtract).then_inc(pooled_ready, 1)
                pool.wait_ge(pooled_ready, g + 1)


        @block.scalar
        def _(s):
            def squares(k):
                for t in range(TT):
                    s.activation(normed[:, t, :], resid[:, t, :], ACT.Square, accum_out=ss[:, k, t:t + 1]).then_inc(sq_done, 1)
                s.wait_ge(sq_done, TT * (k + 1))
                s.activation(ss[:, k, :], ss[:, k, :], ACT.Sqrt, bias=eps[:, 0:1], scale=1.0 / D).then_inc(rms_ready, 1)

            def gain_hi(k):
                for b in (2, 3):
                    s.wait_ge(turned, 4 * k + b + 1)
                    for c in range(2):
                        d = 2 * b + c
                        s.activation(hT[:, d, :], bank[b][:, c * T:(c + 1) * T], ACT.Copy,
                                     scale=col(norms[k], d)).then_inc(hT_hi, 1)

            s.wait_ge(pool_const, 1)
            s.wait_ge(x_loaded, 16)
            squares(0)
            s.wait_ge(vec_ready, 2)
            gain_hi(0)
            for j in range(2):
                s.wait_ge(unit_done, E_IN + 2 * j + 2)
                s.activation(wide[:, j, :], bank[5 + 2 * j][:, :], ACT.Sigmoid).then_inc(sig_ready, 1)
            s.wait_ge(consts, 1)
            for j in range(2):
                s.wait_ge(unit_done, E_IN + 5 + j)
                s.activation(xpad[:, 2 * j:2 * j + 2, PADP:], bank[j][:, :].rearrange("p (c t) -> p c t", c=2),
                             ACT.Copy).then_inc(xpad_ready, 1)
            for g in range(CT):
                s.wait_ge(poolmix_done, g // 2 + 1)
                s.activation(mixT[:, g, :], bank[2 + g // 2][:, (g % 2) * T:(g % 2 + 1) * T], ACT.Copy,
                             scale=col("pool_scale", g)).then_inc(poolT_ready, 1)
            for j in range(CT):
                s.wait_ge(xc_ready, j + 1)
                s.activation(hT[:, j, :], cacc[:, j, :], ACT.Square).then_inc(csq_ready, 1)
            s.wait_ge(cvar_done, 1)
            s.activation(qsq[:, 0, 0:T], bank[5][:, 0:T], ACT.Sqrt, bias=eps[:, 0:1]).then_inc(crms_ready, 1)
            for j in range(CT):
                s.wait_ge(cn_ready, j + 1)
                s.activation(mixT[:, CT + j, :], cacc[:, j, :], ACT.Silu, bias=col("conv_ln_b", j),
                             scale=col("conv_ln_g", j)).then_inc(convT_ready, 1)
            s.wait_ge(resid_ready, 4)
            squares(1)
            gain_hi(1)
            for j in range(FB):
                s.wait_ge(unit_done, ffn_gate[j] + 1)
                if j >= 2:
                    s.wait_ge(hid_ready, j - 1)
                s.activation(wide[:, j % 2, :], bank[4 + j % 2][:, :], ACT.Silu).then_inc(silu_ready, 1)
            s.wait_ge(resid_ready, 8)
            squares(2)
            gain_hi(2)
            s.wait_ge(f_step, 2)
            s.activation(fl[:, 2, :], fl[:, 1, :], ACT.Exp, scale=-1.0).then_inc(f_act, 1)
            s.wait_ge(f_act, 1)
            s.activation(fl[:, 3, :], fl[:, 2, :], ACT.Ln, bias=1.0).then_inc(f_act, 1)
            for m in range(4):
                s.wait_ge(unit_done, O_Q + m + 1)
                s.activation(qsq[:, m, :], bank[4 + m][:, :], ACT.Square).then_inc(qsq_ready, 1)
            for m in range(4):
                s.wait_ge(qms_done, m + 1)
                s.activation(qsq[:, m, :], bank[2 + m % 2][:, :], ACT.Sqrt, bias=eps[:, 0:1]).then_inc(qrms_ready, 1)
            s.wait_ge(unit_done, O_V + 2)
            for t in range(TT):
                s.activation(v[:, t, :], bank[t][:, :], ACT.Copy).then_inc(v_ready, 1)
            for j in range(2):
                s.wait_ge(unit_done, O_SX + j + 1)
                s.activation(sxs[:, 2 * j:2 * j + 2, :], bank[4 + j][:, :].rearrange("p (c t) -> p c t", c=2),
                             ACT.Copy).then_inc(sx_copied, 1)
            for i in range(2 * NH):
                nk = (i % 2 + 1) * P
                s.wait_ge(max_ready, i + 1)
                s.activation(probs[:, i % 2, 0:nk], bank[4 + i % 2][:, 0:nk], ACT.Exp, bias=rmax[:, i, 1:2],
                             accum_out=rmax[:, i, 2:3]).then_inc(exp_ready, 1)
            s.wait_ge(resid_ready, 12)
            squares(3)
            gain_hi(3)
            s.wait_ge(r_step, 3)
            s.activation(lg[:, :, 10, 1], lg[:, :, 10, 0], ACT.Exp).then_inc(r_exp, 1)

            def expert(i, e, group):
                for h in range(2):
                    if h == 1:
                        s.wait_ge(gathered, 1 + i * 2 + 2)
                        for c in range(4):
                            s.activation(xe[:, 4 + c, :], bank[6][:, c * P:(c + 1) * P], ACT.Copy,
                                         scale=col("od_norm_ffn", 4 + c)).then_inc(xe_ready, 1)
                for c in range(EB):
                    s.wait_ge(unit_done, i * PER + MOE + moe_gate[c] + 2)
                    if c >= 2:
                        s.wait_ge(ehid_ready, 1 + i * EB + c - 1)
                    else:
                        s.wait_ge(ehid_ready, 1 + i * EB)
                    s.activation(act[:, c % 2, :], bank[c % 2][:, :], ACT.Silu).then_inc(act_ready, 1)
                s.wait_ge(unit_done, i * PER + MOE + PER)
                s.activation(ye[:, 512:1024], bank[5][:, :], ACT.Copy).then_inc(ye_ready, 1)

            run(s, expert, lambda times: s.nop())

        @block.tensor
        def _(pe):
            def ready(u):
                s, times = slot(u)
                pe.wait_ge(loaded[s], 16 * times)

            def cols_product(u, xT, b):
                ready(u)
                w = view(u, DT, 256)
                for c in range(2):
                    for k in range(DT):
                        mm = pe.matmul(bank[b][:, c * T:(c + 1) * T], w[:, k, c * P:(c + 1) * P], xT[:, k, :],
                                       start=(k == 0), stop=(k == DT - 1))
                mm.then_inc(unit_done, 1)

            def rows_product(u, xT, k0, first, last):
                ready(u)
                w = view(u, 2, D)
                for k in range(2):
                    for t in range(TT):
                        for h in range(2):
                            mm = pe.matmul(bank[2 * t + h][:, :], xT[:, k0 + k, t * P:(t + 1) * P],
                                           w[:, k, h * 512:(h + 1) * 512], start=(first and k == 0), stop=(last and k == 1))
                mm.then_inc(unit_done, 1)

            def turn(k):
                pe.wait_ge(normed_ready, TT * (k + 1))
                for b in range(4):
                    for c in range(2):
                        for t in range(TT):
                            d = 2 * b + c
                            mm = pe.transpose(bank[b][:, c * T + t * P:c * T + (t + 1) * P],
                                              normed[:, t, d * P:(d + 1) * P], ident[:, :])
                    mm.then_inc(turned, 1)

            def out_product(u0, ks):
                for m in ks:
                    rows_product(u0 + m, mixT, 2 * m, m == 0, m == DT // 2 - 1)

            pe.wait_ge(pool_const, 3)
            pe.wait_ge(vectors_loaded, VECTORS)
            pe.transpose(bank[7][:, 0:NV], vrow[0:NV, :], ident[0:NV, 0:NV]).then_inc(vec_turned, 1)
            pe.transpose(bank[6][:, 0:ND], drow[0:ND, :], ident[0:ND, 0:ND]).then_inc(vec_turned, 1)
            turn(0)
            pe.wait_ge(hT_lo, 4)
            pe.wait_ge(hT_hi, 4)
            pe.wait_ge(vec_ready, 2)
            for m, b in enumerate((4, 5, 6, 7, 0, 1)):
                cols_product(E_IN + m, hT, b)
            pe.wait_ge(small_loaded, SMALL)
            for g in range(CT):
                pe.wait_ge(pooled_ready, g + 1)
                w = (winA if g % 2 == 0 else winB)[:, g, PADP:]
                mm = pe.matmul(bank[2 + g // 2][:, (g % 2) * T:(g % 2 + 1) * T], poolw[:, g, :], w, start=True, stop=True)
                if g % 2:
                    mm.then_inc(poolmix_done, 1)
            pe.wait_ge(xpad_ready, 2)
            pe.wait_ge(poolT_ready, CT)
            out_product(E_OUT, range(CT // 2))
            pe.wait_ge(conv_ready, 4)
            pe.wait_ge(u_ready, 2)
            pe.wait_ge(sig_ready, 2)
            for j in range(CT):
                mm = pe.matmul(bank[4][:, 0:T], lnmean[:, :], cacc[:, j, :], start=(j == 0), stop=(j == CT - 1))
            mm.then_inc(mean_done, 1)
            for j in range(CT):
                pe.wait_ge(csq_ready, j + 1)
                mm = pe.matmul(bank[5][:, 0:T], lnmean[:, :], hT[:, j, :], start=(j == 0), stop=(j == CT - 1))
            mm.then_inc(cvar_done, 1)
            pe.wait_ge(convT_ready, CT)
            out_product(E_OUT, range(CT // 2, DT // 2))

            pe.wait_ge(resid_ready, 4)
            turn(1)
            pe.wait_ge(hT_lo, 8)
            pe.wait_ge(hT_hi, 8)
            for j in range(FB + 1):
                if j < FB:
                    if j >= 2:
                        pe.wait_ge(hid_ready, j - 1)
                    cols_product(ffn_gate[j], hT, 4 + j % 2)
                    cols_product(ffn_up[j], hT, 6 + j % 2)
                if j >= 1:
                    pe.wait_ge(hid_ready, j)
                    rows_product(ffn_down[j - 1], hid[:, (j - 1) % 2], 0, j == 1, j == FB)

            pe.wait_ge(resid_ready, 8)
            turn(2)
            pe.wait_ge(hT_lo, 12)
            pe.wait_ge(hT_hi, 12)
            for k in range(DT):
                mm = pe.matmul(bank[2][0:NH, 0:T], wf[:, k, :], hT[:, k, :], start=(k == 0), stop=(k == DT - 1))
            mm.then_inc(f_done, 1)
            for m in range(4):
                cols_product(O_Q + m, hT, 4 + m)
            for u in range(2):
                ready(O_V + u)
                w = view(O_V + u, 4, 512)
                for k in range(4):
                    for t in range(TT):
                        mm = pe.matmul(bank[t][:, :], hT[:, 4 * u + k, t * P:(t + 1) * P], w[:, k, :],
                                       start=(u == 0 and k == 0), stop=(u == 1 and k == 3))
                mm.then_inc(unit_done, 1)
            pe.wait_ge(f_step, 1)
            for m in range(4):
                pe.wait_ge(qsq_ready, m + 1)
                if m >= 2:
                    pe.wait_ge(qrms_ready, m - 1)
                pe.matmul(bank[2 + m % 2][:, :], headmean[:, :], qsq[:, m, :], start=True, stop=True).then_inc(qms_done, 1)
            for m, b in enumerate((4, 5, 6, 7, 0, 1)):
                if m < 4:
                    pe.wait_ge(qk_ready, m + 1)
                else:
                    pe.wait_ge(v_ready, TT)
                cols_product(O_SX + m, hT, b)

            pe.wait_ge(f_ready, 2)
            pe.wait_ge(sx_copied, 2)
            pe.wait_ge(z_ready, 2)
            pe.wait_ge(qrms_ready, 4)

            def scores(i):
                h, q = i // 2, i % 2
                nk, r = (q + 1) * P, (h % 2) * HD
                b = bank[4 + i % 2]
                if i >= 2:
                    pe.wait_ge(exp_ready, i - 1)
                qh = qkT[r:r + HD, h // 4, (h // 2) % 2, q * P:(q + 1) * P]
                kh = qkT[r:r + HD, 2 + h // 4, (h // 2) % 2, 0:nk]
                pe.matmul(b[:, 0:nk], qh, kh, start=True, stop=False)
                pe.matmul(b[:, nk - P:nk], ident[:, :], causal[:, :], start=False, stop=False)
                pe.matmul(b[:, 0:nk], fl[:, 4, q * P:(q + 1) * P], sel[:, h, 0:nk], start=False, stop=False)
                pe.matmul(b[:, 0:nk], sel[:, h, 0:P], fl[:, 5, 0:nk], start=False, stop=True).then_inc(score_done, 1)

            def turn_probs(i):
                nk = (i % 2 + 1) * P
                pe.wait_ge(p_ready, i + 1)
                if i >= 2:
                    pe.wait_ge(pT_ready, i - 1)
                for c in range(nk // P):
                    mm = pe.transpose(bank[6 + i % 2][:, c * P:(c + 1) * P], probs[:, i % 2, c * P:(c + 1) * P], ident[:, :])
                mm.then_inc(pT_done, 1)

            def attend(i):
                h, q = i // 2, i % 2
                r = (h % 2) * HD
                pe.wait_ge(pT_ready, i + 1)
                if i >= 2:
                    pe.wait_ge(o_copied, i - 1)
                for c in range(q + 1):
                    mm = pe.matmul(bank[2 + i % 2][r:r + HD, 0:P], v[:, c, h * HD:(h + 1) * HD],
                                   probsT[:, i % 2, c * P:(c + 1) * P], start=(c == 0), stop=(c == q))
                mm.then_inc(o_done, 1)

            for i in range(2 * NH + 2):
                if i < 2 * NH:
                    scores(i)
                if 1 <= i <= 2 * NH:
                    turn_probs(i - 1)
                if i >= 2:
                    attend(i - 2)
            pe.wait_ge(o_copied, 2 * NH)
            pe.wait_ge(shortT_ready, CT)
            out_product(O_OUT, range(DT // 2))

            pe.wait_ge(resid_ready, 12)
            turn(3)
            pe.wait_ge(hT_lo, 16)
            pe.wait_ge(hT_hi, 16)
            for t in range(TT):
                for k in range(DT):
                    mm = pe.matmul(bank[4 + t][:, 0:NE], hT[:, k, t * P:(t + 1) * P], wr[:, k, :],
                                   start=(k == 0), stop=(k == DT - 1))
                mm.then_inc(logits_done, 1)
            pe.wait_ge(mask_ready, 1)
            pe.matmul(bank[6][:, 0:NE], before[:, :], lg[:, 0, 8, :], start=True, stop=True).then_inc(count_done, 1)
            pe.matmul(bank[7][:, 0:NE], ones[:, 0:P], lg[:, 0, 8, :], start=True, stop=False)
            pe.matmul(bank[7][:, 0:NE], before[:, :], lg[:, 1, 8, :], start=False, stop=True).then_inc(count_done, 1)
            pe.matmul(bank[5][:, 0:NE], ones[:, 0:P], lg[:, 0, 8, :], start=True, stop=False)
            pe.matmul(bank[5][:, 0:NE], ones[:, 0:P], lg[:, 1, 8, :], start=False, stop=True).then_inc(count_done, 1)
            pe.wait_ge(route_ready, 1)

            for free in (gathered, dispT_done, ehidT_done):
                pe.sem_inc(free, 1)

            def expert(i, e, group):
                pe.wait_ge(disp_ready, i * 2 * TT + 2 * TT)
                pe.wait_ge(added, 1 + i * 4)
                for h in range(2):
                    for c in range(4):
                        for t in range(TT):
                            d = 4 * h + c
                            mm = pe.matmul(bank[7 - h][:, c * P:(c + 1) * P], normed[:, t, d * P:(d + 1) * P],
                                           disp[:, t, :], start=(t == 0), stop=(t == TT - 1))
                    mm.then_inc(gathered, 1)
                pe.wait_ge(xe_ready, i * DT + DT)
                for t in range(TT):
                    mm = pe.transpose(bank[7][:, t * P:(t + 1) * P], dispw[:, t, :], ident[:, :])
                mm.then_inc(dispT_done, 1)

                def up_product(j, b):
                    for h in range(2):
                        u = MOE + j + h
                        s, times = slot(u)
                        pe.wait_ge(loaded[s], i * (16 * (PER // RING)) + 16 * times)
                        w = view(u, 4, 512)
                        for k in range(4):
                            mm = pe.matmul(bank[b][:, :], xe[:, 4 * h + k, :], w[:, k, :], start=(h == 0 and k == 0),
                                           stop=(h == 1 and k == 3))
                        mm.then_inc(unit_done, 1)

                for c in range(EB + 1):
                    if c < EB:
                        pe.wait_ge(ehid_ready, 1 + i * EB + max(c - 1, 0))
                        up_product(moe_gate[c], c % 2)
                    if c >= 1:
                        pe.wait_ge(ehid_ready, 1 + i * EB + c)
                        pe.wait_ge(ehidT_ready, 1 + i * EB + c - 1)
                        for f in range(4):
                            mm = pe.transpose(bank[6][:, f * P:(f + 1) * P], ehid[:, (c - 1) % 2, f * P:(f + 1) * P],
                                              ident[:, :])
                        mm.then_inc(ehidT_done, 1)
                    if c < EB:
                        up_product(moe_up[c], 2 + c % 2)
                    if c >= 1:
                        pe.wait_ge(ehidT_ready, 1 + i * EB + c)
                        if c == 1:
                            pe.wait_ge(ye_ready, 1 + i * 2)
                        for h in range(2):
                            u = MOE + moe_down[c - 1] + h
                            s, times = slot(u)
                            pe.wait_ge(loaded[s], i * (16 * (PER // RING)) + 16 * times)
                            w = view(u, 2, D)
                            for k in range(2):
                                for n_ in range(2):
                                    mm = pe.matmul(bank[4 + n_][:, :], ehidT[:, (c - 1) % 2, 2 * h + k, :],
                                                   w[:, k, n_ * 512:(n_ + 1) * 512], start=(c == 1 and h == 0 and k == 0),
                                                   stop=(c == EB and h == 1 and k == 1))
                            mm.then_inc(unit_done, 1)
                pe.wait_ge(dispT_ready, i + 1)
                pe.wait_ge(ye_ready, 1 + i * 2 + 2)
                for t in range(TT):
                    for h in range(2):
                        if t >= 1:
                            pe.wait_ge(added, 1 + i * 4 + (t - 1) * 2 + h + 1)
                        pe.matmul(bank[6 + h][:, :], dispT[:, t, :], ye[:, h * 512:(h + 1) * 512],
                                  start=True, stop=True).then_inc(scattered, 1)

            run(pe, expert, lambda times: pe.nop())

        @block.vector
        def _(d):
            for g, w in enumerate(WINDOWS):
                if g == 0:
                    d.wait_ge(pool_const, 4)
                d.tensor_scalar(rcount[:, g, :], iota[:, :], 1.0, float(w), ALU.add, ALU.min).then_inc(dve_const, 1)
            for g in range(CT):
                d.wait_ge(dve_const, g + 1)
                d.reciprocal(rcount[:, g, :], rcount[:, g, :]).then_inc(dve_const, 1)
            d.wait_ge(vec_turned, 2)
            d.tensor_copy(vcol[:, 0:NV], bank[7][:, 0:NV]).then_inc(vec_ready, 1)
            d.tensor_copy(dcol[:, 0:ND], bank[6][:, 0:ND]).then_inc(vec_ready, 1)

            def normalize(k):
                d.wait_ge(rms_ready, k + 1)
                d.reciprocal(rstd[:, k, :], ss[:, k, :]).then_inc(rstd_ready, 1)
                d.wait_ge(rstd_ready, k + 1)
                for t in range(TT):
                    d.tensor_scalar(normed[:, t, :], resid[:, t, :], rstd[:, k, t:t + 1], None, ALU.mult).then_inc(normed_ready, 1)

            def gain_lo(k):
                for b in (0, 1):
                    d.wait_ge(turned, 4 * k + b + 1)
                    for c in range(2):
                        n = 2 * b + c
                        d.tensor_scalar(hT[:, n, :], bank[b][:, c * T:(c + 1) * T], col(norms[k], n), None,
                                        ALU.mult).then_inc(hT_lo, 1)

            def residual(u, k):
                d.wait_ge(unit_done, u)
                for t in range(TT):
                    for h in range(2):
                        r = resid[:, t, h * 512:(h + 1) * 512]
                        d.tensor_tensor(r, r, bank[2 * t + h][:, :], ALU.add).then_inc(resid_ready, 1)

            d.wait_ge(x_loaded, 16)
            normalize(0)
            d.wait_ge(vec_ready, 2)
            gain_lo(0)
            d.wait_ge(consts, 2)
            for j in range(2):
                d.wait_ge(sig_ready, j + 1)
                d.tensor_tensor(upad[:, 2 * j:2 * j + 2, PADC:], bank[4 + 2 * j][:, :].rearrange("p (c t) -> p c t", c=2),
                                wide[:, j, :].rearrange("p (c t) -> p c t", c=2), ALU.mult).then_inc(u_ready, 1)
            for s_ in range(TAPS):
                for j in range(CT):
                    w = dcol[:, s_ * CT + j:s_ * CT + j + 1]
                    src = upad[:, j, s_:s_ + T]
                    if s_ == 0:
                        d.wait_ge(u_ready, j // 2 + 1)
                        ins = d.tensor_scalar(cacc[:, j, :], src, w, col("conv_dw_b", j), ALU.mult, ALU.add)
                    else:
                        d.wait_ge(conv_step, (s_ - 1) * CT + j + 1)
                        ins = d.scalar_tensor_tensor(out=cacc[:, j, :], in0=src, scalar=w, in1=cacc[:, j, :],
                                                     op0=ALU.mult, op1=ALU.add)
                    ins.then_inc(conv_ready if s_ == TAPS - 1 else conv_step, 1)
            d.wait_ge(mean_done, 1)
            for j in range(CT):
                d.wait_ge(conv_ready, j + 1)
                d.tensor_tensor(cacc[:, j, :], cacc[:, j, :], bank[4][:, 0:T], ALU.subtract).then_inc(xc_ready, 1)
            d.wait_ge(crms_ready, 1)
            d.reciprocal(qsq[:, 1, 0:T], qsq[:, 0, 0:T]).then_inc(crstd_ready, 1)
            d.wait_ge(crstd_ready, 1)
            for j in range(CT):
                d.wait_ge(xc_ready, j + 1)
                d.wait_ge(csq_ready, j + 1)
                d.tensor_tensor(cacc[:, j, :], cacc[:, j, :], qsq[:, 1, 0:T], ALU.mult).then_inc(cn_ready, 1)
            residual(FFN, 0)
            normalize(1)
            gain_lo(1)
            for j in range(FB):
                d.wait_ge(silu_ready, j + 1)
                d.wait_ge(unit_done, ffn_up[j] + 1)
                if j >= 2:
                    d.wait_ge(unit_done, ffn_down[j - 2] + 1)
                d.tensor_tensor(hid[:, j % 2, :, :], wide[:, j % 2, :].rearrange("p (c t) -> p c t", c=2),
                                bank[6 + j % 2][:, :].rearrange("p (c t) -> p c t", c=2), ALU.mult).then_inc(hid_ready, 1)
            residual(O_IN, 1)
            normalize(2)
            gain_lo(2)
            d.wait_ge(f_done, 1)
            d.wait_ge(small_loaded, SMALL)
            d.tensor_scalar(fl[:, 0, :], bank[2][0:NH, 0:T], fb[:, 0:1], None, ALU.add).then_inc(f_step, 1)
            d.wait_ge(f_step, 1)
            d.scalar_tensor_tensor(out=fl[:, 1, :], in0=fl[:, 0, :], scalar=-1.0, in1=fl[:, 0, :], op0=ALU.mult,
                                   op1=ALU.max).then_inc(f_step, 1)
            d.wait_ge(f_act, 2)
            d.scalar_tensor_tensor(out=fl[:, 0, :], in0=fl[:, 0, :], scalar=0.0, in1=fl[:, 3, :], op0=ALU.min,
                                   op1=ALU.subtract).then_inc(f_step, 1)
            d.wait_ge(f_step, 3)
            d.tensor_tensor_scan(fl[:, 4, :], ones[0:NH, :], fl[:, 0, :], 0.0, ALU.mult, ALU.add).then_inc(f_ready, 1)
            d.wait_ge(f_ready, 1)
            d.tensor_scalar(fl[:, 5, :], fl[:, 4, :], -1.0, None, ALU.mult).then_inc(f_ready, 1)
            d.tensor_scalar(qkg[:, 0:1], qkg[:, 0:1], float(HD) ** -0.5, None, ALU.mult).then_inc(f_ready, 1)
            for m in range(4):
                d.wait_ge(qrms_ready, m + 1)
                d.reciprocal(qsq[:, m, :], qsq[:, m, :]).then_inc(qrstd_ready, 1)
            d.wait_ge(f_ready, 3)
            for m in range(4):
                d.wait_ge(qrstd_ready, m + 1)
                d.scalar_tensor_tensor(out=qkT[:, m, :, :].rearrange("p c t -> p (c t)"), in0=bank[4 + m][:, :],
                                       scalar=qkg[:, m // 2:m // 2 + 1], in1=qsq[:, m, :], op0=ALU.mult,
                                       op1=ALU.mult).then_inc(qk_ready, 1)
            d.wait_ge(consts, 5)
            for j in range(2):
                d.wait_ge(unit_done, O_SC + j + 1)
                d.wait_ge(sx_copied, j + 1)
                d.tensor_tensor(spad[:, 2 * j:2 * j + 2, PADS:], bank[6 + j][:, :].rearrange("p (c t) -> p c t", c=2),
                                sxs[:, 2 * j:2 * j + 2, :], ALU.mult).then_inc(z_ready, 1)
            short = []
            for s_ in range(STAPS):
                for j in range(CT):
                    short.append((s_, j))

            def short_tap(s_, j):
                w = vcol[:, SCW + s_ * CT + j:SCW + s_ * CT + j + 1]
                src = spad[:, j, s_:s_ + T]
                if s_ == 0:
                    d.wait_ge(z_ready, j // 2 + 1)
                    ins = d.tensor_scalar(sacc[:, j, :], src, w, None, ALU.mult)
                else:
                    d.wait_ge(s_step, (s_ - 1) * CT + j + 1)
                    ins = d.scalar_tensor_tensor(out=sacc[:, j, :], in0=src, scalar=w, in1=sacc[:, j, :],
                                                 op0=ALU.mult, op1=ALU.add)
                ins.then_inc(s_step, 1)

            def short_gate(j):
                d.wait_ge(unit_done, O_SB + 2)
                d.wait_ge(s_step, (STAPS - 1) * CT + j + 1)
                d.tensor_tensor(mixT[:, CT + j, :], sacc[:, j, :], bank[j // 2][:, (j % 2) * T:(j % 2 + 1) * T],
                                ALU.mult).then_inc(shortT_ready, 1)

            def softmax_max(i):
                nk = (i % 2 + 1) * P
                d.wait_ge(score_done, i + 1)
                d.tensor_reduce(rmax[:, i, 0:1], bank[4 + i % 2][:, 0:nk], AX.X, ALU.max).then_inc(max_step, 1)
                d.wait_ge(max_step, i + 1)
                d.tensor_scalar(rmax[:, i, 1:2], rmax[:, i, 0:1], -1.0, None, ALU.mult).then_inc(max_ready, 1)

            def softmax_norm(i):
                nk = (i % 2 + 1) * P
                d.wait_ge(exp_ready, i + 1)
                d.reciprocal(rmax[:, i, 3:4], rmax[:, i, 2:3]).then_inc(p_step, 1)
                d.wait_ge(p_step, i + 1)
                d.tensor_scalar(probs[:, i % 2, 0:nk], probs[:, i % 2, 0:nk], rmax[:, i, 3:4], None,
                                ALU.mult).then_inc(p_ready, 1)

            def copy_pT(i):
                nk = (i % 2 + 1) * P
                d.wait_ge(pT_done, i + 1)
                d.tensor_copy(probsT[:, i % 2, 0:nk], bank[6 + i % 2][:, 0:nk]).then_inc(pT_ready, 1)

            def copy_o(i):
                h, q = i // 2, i % 2
                r = (h % 2) * HD
                d.wait_ge(o_done, i + 1)
                d.tensor_copy(mixT[r:r + HD, h // 2, q * P:(q + 1) * P], bank[2 + i % 2][r:r + HD, 0:P]).then_inc(o_copied, 1)

            for i in range(2 * NH + 2):
                if i < 2 * NH:
                    softmax_max(i)
                    softmax_norm(i)
                if 1 <= i <= 2 * NH:
                    copy_pT(i - 1)
                if i >= 2:
                    copy_o(i - 2)
                if i < len(short):
                    short_tap(*short[i])
                elif i < len(short) + CT:
                    short_gate(i - len(short))
            residual(MOE, 2)
            normalize(3)
            gain_lo(3)

            r = [0]

            def chain(ins):
                r[0] += 1
                ins.then_inc(r_step, 1)
                d.wait_ge(r_step, r[0])

            d.wait_ge(logits_done, TT)
            for t in range(TT):
                ins = d.tensor_tensor(lg[:, t, 0, :], bank[4 + t][:, 0:NE], rb[:, :], ALU.add)
                if t == 0:
                    ins.then_inc(max_step, 1)
            d.wait_ge(max_step, 2 * NH + 1)
            chain(ins)
            for t in range(TT):
                ins = d.max(lg[:, t, 1, :], lg[:, t, 0, :])
                if t == 0:
                    ins.then_inc(max_step, 1)
            d.wait_ge(max_step, 2 * NH + 2)
            chain(ins)
            chain(d.tensor_tensor(lg[:, :, 10, 0], lg[:, :, 1, 1], lg[:, :, 1, 0], ALU.subtract))
            for t in range(TT):
                chain(d.max_index(idx[:, t, :], lg[:, t, 1, :], lg[:, t, 0, :]))
            chain(d.tensor_copy(lg[:, :, 2, 0:2], idx[:, :, 0:2]))
            for t in range(TT):
                for k in range(2):
                    chain(d.tensor_scalar(lg[:, t, 3 + k, :], iota[:, 0:NE], lg[:, t, 2, k:k + 1], None, ALU.is_equal))
            chain(d.tensor_tensor(lg[:, :, 8, :], lg[:, :, 3, :], lg[:, :, 4, :], ALU.add))
            d.wait_ge(r_exp, 1)
            d.tensor_scalar(lg[:, :, 10, 2], lg[:, :, 10, 1], 1.0, None, ALU.add).then_inc(mask_ready, 1)
            d.wait_ge(mask_ready, 1)
            chain(d.reciprocal(lg[:, :, 10, 3], lg[:, :, 10, 2]))
            chain(d.tensor_tensor(lg[:, :, 10, 4], lg[:, :, 10, 3], lg[:, :, 10, 1], ALU.mult))
            for t in range(TT):
                chain(d.tensor_scalar(lg[:, t, 5, :], lg[:, t, 3, :], lg[:, t, 10, 3:4], None, ALU.mult))
                chain(d.scalar_tensor_tensor(out=comb[:, t, :], in0=lg[:, t, 4, :], scalar=lg[:, t, 10, 4:5],
                                             in1=lg[:, t, 5, :], op0=ALU.mult, op1=ALU.add))
            d.wait_ge(count_done, 3)
            for t in range(TT):
                chain(d.scalar_tensor_tensor(out=lg[:, t, 6, :], in0=bank[6 + t][:, 0:NE], scalar=1.0,
                                             in1=lg[:, t, 8, :], op0=ALU.add, op1=ALU.mult))
            chain(d.tensor_scalar(pos[:, 0, :, :], lg[:, :, 6, :], -1.0, None, ALU.add))
            chain(d.tensor_scalar(pos[:, 1, :, :], lg[:, :, 6, :], -1.0 - P, None, ALU.add))
            chain(d.tensor_reduce(cnt[:, 0:1], bank[5][:, 0:NE], AX.X, ALU.max))
            chain(d.tensor_scalar(cnt[:, 1:2], cnt[:, 0:1], float(P), None, ALU.is_gt))
            d.tensor_copy(over[:, :], cnt[:, 1:2]).then_inc(over_ready, 1)
            d.wait_ge(over_ready, 1)
            d.tensor_copy(cnt[:, 0:1], cnt[:, 1:2]).then_inc(route_ready, 1)

            for free in (added, ehid_ready, ehidT_ready, ye_ready):
                d.sem_inc(free, 1)

            def expert(i, e, group):
                d.wait_ge(gathered, 1 + i * 2)
                d.wait_ge(dispT_done, 1 + i)
                for t in range(TT):
                    where = pos[:, group, t, bass.ds(e, 1)]
                    d.tensor_scalar(disp[:, t, :], iota[:, 0:P], where, None, ALU.is_equal).then_inc(disp_ready, 1)
                    d.tensor_scalar(dispw[:, t, :], iota[:, 0:P], where, comb[:, t, bass.ds(e, 1)], ALU.is_equal,
                                    ALU.mult).then_inc(disp_ready, 1)
                d.wait_ge(gathered, 1 + i * 2 + 1)
                for c in range(4):
                    d.tensor_scalar(xe[:, c, :], bank[7][:, c * P:(c + 1) * P], col("od_norm_ffn", c), None,
                                    ALU.mult).then_inc(xe_ready, 1)
                d.wait_ge(dispT_done, 1 + i + 1)
                d.tensor_copy(dispT[:, :, :], bank[7][:, 0:TT * P].rearrange("p (t s) -> p t s", t=TT)).then_inc(dispT_ready, 1)
                for c in range(EB + 1):
                    if c < EB:
                        d.wait_ge(act_ready, i * EB + c + 1)
                        d.wait_ge(unit_done, i * PER + MOE + moe_up[c] + 2)
                        d.wait_ge(ehidT_done, 1 + i * EB + max(c - 1, 0))
                        d.tensor_tensor(ehid[:, c % 2, :], act[:, c % 2, :], bank[2 + c % 2][:, :], ALU.mult).then_inc(ehid_ready, 1)
                    if c >= 1:
                        d.wait_ge(ehidT_done, 1 + i * EB + c)
                        d.tensor_copy(ehidT[:, (c - 1) % 2, :, :], bank[6][:, :].rearrange("p (f s) -> p f s", f=4)).then_inc(ehidT_ready, 1)
                d.wait_ge(unit_done, i * PER + MOE + PER)
                d.tensor_copy(ye[:, 0:512], bank[4][:, :]).then_inc(ye_ready, 1)
                for t in range(TT):
                    for h in range(2):
                        d.wait_ge(scattered, i * 4 + 2 * t + h + 1)
                        r_ = resid[:, t, h * 512:(h + 1) * 512]
                        d.tensor_tensor(r_, r_, bank[6 + h][:, :], ALU.add).then_inc(added, 1)

            def finish(times):
                d.wait_ge(added, 1 + 4 * NE * times)
                d.tensor_copy(cnt[:, 0:1], cnt[:, 1:2]).then_inc(out_ready, 1)

            run(d, expert, finish)


def kernel(**inputs):
    import numpy as np
    import concourse.bacc as bacc
    from concourse.bass_utils import run_bass_kernel_spmd

    nc = bacc.Bacc("TRN2", target_bir_lowering=False, num_devices=1)
    arrays, args = {}, {}
    for name, value in inputs.items():
        value = np.ascontiguousarray(value)
        arrays[f"in_{name}"] = value
        args[name] = nc.dram_tensor(f"in_{name}", value.shape, mybir.dt.from_np(value.dtype), kind="ExternalInput").ap()
    shape = inputs["x"].shape
    result = nc.dram_tensor("out_x", shape, F32, kind="ExternalOutput").ap()
    build_trunk(nc, args, result)
    ran = run_bass_kernel_spmd(nc, [arrays], core_ids=[0])
    return ran.results[0]["out_x"]
```

```python
from contextlib import ExitStack

import concourse.bass as bass
from concourse import mybir

F32 = mybir.dt.float32
F32R = mybir.dt.float32r
I32 = mybir.dt.int32
ALU = mybir.AluOpType
ACT = mybir.ActivationFunctionType
AX = mybir.AxisListType

P = 128
UNIT = 2048
RING = 14
HALF = UNIT // 2
SPLITS = 4
AHEAD = 3
EPS = 1e-6
WINDOWS = (2, 4, 8, 16)
NEG = -1.0e30


def build_trunk(nc, a, out):
    T, D = a["x"].shape[1:]
    TT, DT = T // P, D // P
    C = a["pool_scale"].shape[1]
    CT = C // P
    TAPS = a["conv_dw_w"].shape[1]
    STAPS = a["sc_conv_w"].shape[1]
    F = a["ffn_w_gate"].shape[2]
    NH = a["forget_bias"].shape[1]
    HD = a["q_norm_g"].shape[1]
    NE = a["router_w"].shape[2]
    FE = a["moe_w_gate"].shape[3]
    PADC, PADS, PADP = TAPS - 1, STAPS - 1, max(WINDOWS) - 1
    FB = F // 256
    EB = FE // 512

    def cols_unit(w, c0):
        return w[:, c0:c0 + 256].rearrange("(k p) n -> p k n", p=P), DT, 256

    def half_unit(w, k0, c0):
        return w[k0 * P:(k0 + 4) * P, c0:c0 + 512].rearrange("(k p) n -> p k n", p=P), 4, 512

    def rows_unit(w, k0):
        return w[k0 * P:(k0 + 2) * P, :].rearrange("(k p) n -> p k n", p=P), 2, D

    ev_in, od_in = a["ev_w_in"][0], a["od_w_in"][0]
    wg, wu, wd = a["ffn_w_gate"][0], a["ffn_w_up"][0], a["ffn_w_down"][0]
    units = [cols_unit(ev_in, c) for c in (C, 2 * C, C + 256, 2 * C + 256, 0, 256)]
    E_IN = 0
    E_OUT = len(units)
    units += [rows_unit(a["ev_w_out"][0], 2 * m) for m in range(DT // 2)]
    FFN = len(units)
    ffn_gate, ffn_up, ffn_down = {}, {}, {}
    for j in range(FB + 1):
        if j < FB:
            ffn_gate[j] = len(units)
            units.append(cols_unit(wg, 256 * j))
            ffn_up[j] = len(units)
            units.append(cols_unit(wu, 256 * j))
        if j >= 1:
            ffn_down[j - 1] = len(units)
            units.append(rows_unit(wd, 2 * (j - 1)))
    O_IN = len(units)
    S0 = 3 * C + NH
    units += [cols_unit(od_in, c) for c in (0, 256, C, C + 256)]
    units += [half_unit(od_in, k, 2 * C) for k in (0, 4)]
    units += [cols_unit(od_in, S0 + c) for c in (0, 256, 2 * C, 2 * C + 256, C, C + 256)]
    O_Q, O_K, O_V, O_SX, O_SC, O_SB = O_IN, O_IN + 2, O_IN + 4, O_IN + 6, O_IN + 8, O_IN + 10
    O_OUT = len(units)
    units += [rows_unit(a["od_w_out"][0], 2 * m) for m in range(DT // 2)]
    MOE = len(units)
    moe_gate, moe_up, moe_down, PER = {}, {}, {}, 0
    expert_units = []
    for c in range(EB + 1):
        if c < EB:
            moe_gate[c], moe_up[c] = PER, PER + 2
            expert_units += [("moe_w_gate", 4 * h, 512 * c) for h in (0, 1)]
            expert_units += [("moe_w_up", 4 * h, 512 * c) for h in (0, 1)]
            PER += 4
        if c >= 1:
            moe_down[c - 1] = PER
            expert_units += [("moe_w_down", 4 * (c - 1) + 2 * h, None) for h in (0, 1)]
            PER += 2
    assert PER == len(expert_units) and PER % RING == 0

    with ExitStack() as ctx:
        def sb(name, shape, dt=F32):
            return ctx.enter_context(nc.sbuf_tensor(name, shape, dt))

        def sem(name):
            return ctx.enter_context(nc.semaphore(name))

        ring = sb("ring", [P, RING, UNIT])
        whi = sb("whi", [P, SPLITS, HALF], F32R)
        wlo = sb("wlo", [P, SPLITS, HALF], F32R)
        resid = sb("resid", [P, TT, D])
        normed = sb("normed", [P, TT, D])
        xhi = sb("xhi", [P, DT, T], F32R)
        xlo = sb("xlo", [P, DT, T], F32R)
        hhi = sb("hhi", [P, 2, 512], F32R)
        hlo = sb("hlo", [P, 2, 512], F32R)

        ARENA = 6960
        arena = sb("arena", [P, ARENA])

        class Phase:
            def __init__(self):
                self.at = 0

            def take(self, *dims):
                n = 1
                for x in dims:
                    n *= x
                flat = arena[:, self.at:self.at + n]
                self.at += n
                assert self.at <= ARENA
                if len(dims) == 1:
                    return flat
                if len(dims) == 2:
                    return flat.rearrange("p (a b) -> p a b", a=dims[0])
                return flat.rearrange("p (a b c) -> p a b c", a=dims[0], b=dims[1])

        even = Phase()
        upad = even.take(CT, PADC + T)
        cacc = even.take(CT, T)
        xpad = even.take(CT, PADP + T)
        winA = even.take(CT, PADP + T)
        winB = even.take(CT, PADP + T)
        rcount = even.take(CT, T)
        poolw = even.take(CT, P)
        csq = rcount
        crms = xpad[:, 0:2, 0:T]
        sig = winA.rearrange("p a b -> p (a b)")[:, 0:1024].rearrange("p (a b) -> p a b", a=2)
        ffn = Phase()
        gated = ffn.take(2, 512)
        hidden = ffn.take(2, 512)
        odd = Phase()
        qkT = odd.take(4, 2, T)
        qsq = normed[:, :, :].rearrange("p t (m n) -> p (t m) n", n=512)
        v = odd.take(TT, C)
        fl = odd.take(4, T)
        probs = odd.take(2, T)
        probsT = odd.take(2, T)
        spad = odd.take(CT, PADS + T)
        sxs = qsq[:, 0:2, :].rearrange("p a (c t) -> p (a c) t", c=2)
        sacc = qsq[:, 2:4, :].rearrange("p a (c t) -> p (a c) t", c=2)
        moe = Phase()
        hrT = moe.take(DT, T)
        grow = moe.take(D)
        disp = moe.take(TT, P)
        dispw = moe.take(TT, P)
        dispT = moe.take(TT, P)
        act = hrT[:, 0:4, :].rearrange("p (a b) t -> p a (b t)", a=2)
        ehid = hrT[:, 4:8, :].rearrange("p (a b) t -> p a (b t)", a=2)
        ye = grow
        lg = moe.take(TT, 12, NE)

        ss = sb("ss", [P, 4, TT])
        rstd = sb("rstd", [P, 4, TT])
        vrow = sb("vrow", [P, P])
        drow = sb("drow", [P, P])
        vcol = sb("vcol", [P, P])
        dcol = sb("dcol", [P, P])
        ident = sb("ident", [P, P])
        ones = sb("ones", [P, T])
        headmean = sb("headmean", [P, P])
        lnmean = sb("lnmean", [P, P])
        before = sb("before", [P, P])
        causal = sb("causal", [P, P])
        eps = sb("eps", [P, 1])
        iota = sb("iota", [P, T])
        qkg = sb("qkg", [P, 2])
        fb = sb("fb", [NH, 1])
        wf = sb("wf", [P, DT, NH])
        wr = sb("wr", [P, DT, NE])
        rb = sb("rb", [P, NE])
        rmax = sb("rmax", [P, 2 * NH, 4])
        idx = sb("idx", [P, TT, 8], mybir.dt.uint32)
        pos = sb("pos", [P, TT, 2 * NE + 1])
        comb = sb("comb", [P, TT, 2 * NE + 1])
        cnt = sb("cnt", [P, 2])
        over = sb("over", [P, 1], I32)

        bank = [ctx.enter_context(nc.psum_tensor(f"bank{i}", [P, 512], F32)) for i in range(8)]

        loaded = [sem(f"loaded{s}") for s in range(RING)]
        hi_ready = sem("hi_ready")
        lo_ready = sem("lo_ready")
        half_done = sem("half_done")
        vectors_loaded = sem("vectors_loaded")
        small_loaded = sem("small_loaded")
        grow_loaded = sem("grow_loaded")
        x_loaded = sem("x_loaded")
        pool_const = sem("pool_const")
        consts = sem("consts")
        dve_const = sem("dve_const")
        vec_turned = sem("vec_turned")
        vec_ready = sem("vec_ready")
        sq_done = sem("sq_done")
        rms_ready = sem("rms_ready")
        rstd_ready = sem("rstd_ready")
        normed_ready = sem("normed_ready")
        turned = sem("turned")
        xhi_ready = sem("xhi_ready")
        xlo_ready = sem("xlo_ready")
        sig_ready = sem("sig_ready")
        u_ready = sem("u_ready")
        xpad_ready = sem("xpad_ready")
        pool_step = sem("pool_step")
        pooled_ready = sem("pooled_ready")
        poolmix_done = sem("poolmix_done")
        conv_step = sem("conv_step")
        conv_ready = sem("conv_ready")
        mean_done = sem("mean_done")
        xc_ready = sem("xc_ready")
        csq_ready = sem("csq_ready")
        cvar_done = sem("cvar_done")
        crms_ready = sem("crms_ready")
        crstd_ready = sem("crstd_ready")
        cn_ready = sem("cn_ready")
        cout_ready = sem("cout_ready")
        resid_ready = sem("resid_ready")
        silu_ready = sem("silu_ready")
        hid_ready = sem("hid_ready")
        hhi_ready = sem("hhi_ready")
        hlo_ready = sem("hlo_ready")
        f_done = sem("f_done")
        f_step = sem("f_step")
        f_act = sem("f_act")
        f_ready = sem("f_ready")
        qsq_ready = sem("qsq_ready")
        qms_done = sem("qms_done")
        qrms_ready = sem("qrms_ready")
        qrstd_ready = sem("qrstd_ready")
        qk_ready = sem("qk_ready")
        v_ready = sem("v_ready")
        sx_copied = sem("sx_copied")
        s_step = sem("s_step")
        z_ready = sem("z_ready")
        short_ready = sem("short_ready")
        short_hi = sem("short_hi")
        short_lo = sem("short_lo")
        score_done = sem("score_done")
        max_step = sem("max_step")
        max_ready = sem("max_ready")
        exp_ready = sem("exp_ready")
        p_step = sem("p_step")
        p_ready = sem("p_ready")
        pT_done = sem("pT_done")
        pT_ready = sem("pT_ready")
        o_done = sem("o_done")
        o_hi = sem("o_hi")
        o_lo = sem("o_lo")
        hr_lo = sem("hr_lo")
        hr_hi = sem("hr_hi")
        logits_done = sem("logits_done")
        r_step = sem("r_step")
        r_exp = sem("r_exp")
        mask_ready = sem("mask_ready")
        count_done = sem("count_done")
        over_ready = sem("over_ready")
        disp_ready = sem("disp_ready")
        gathered = sem("gathered")
        ehi_ready = sem("ehi_ready")
        elo_ready = sem("elo_ready")
        dispT_done = sem("dispT_done")
        dispT_ready = sem("dispT_ready")
        act_ready = sem("act_ready")
        ehid_ready = sem("ehid_ready")
        ehidT_done = sem("ehidT_done")
        ehidT_hi = sem("ehidT_hi")
        ehidT_lo = sem("ehidT_lo")
        ye_ready = sem("ye_ready")
        scattered = sem("scattered")
        added = sem("added")
        out_ready = sem("out_ready")
        out_stored = sem("out_stored")

        rows, n = {}, 0
        for name, k in (("ev_norm_mix", DT), ("ev_norm_ffn", DT), ("od_norm_mix", DT),
                        ("pool_scale", CT), ("conv_dw_b", CT), ("conv_ln_g", CT), ("conv_ln_b", CT)):
            rows[name] = (n, k)
            n += k
        SCW = n
        NV = n + STAPS * CT
        ND = TAPS * CT

        def col(name, k):
            i = rows[name][0] + k
            return vcol[:, i:i + 1]

        norms = ("ev_norm_mix", "ev_norm_ffn", "od_norm_mix")
        VECTORS, SMALL = 16 * (len(rows) + 2), 16 * 9

        def view(u, k):
            return ring[:, u % RING, :].rearrange("p (k n) -> p k n", k=k)

        def half_shape(u):
            k = (units[u] if u < MOE else (None, (4 if expert_units[(u - MOE) % PER][2] is not None else 2)))[1]
            return (DT, P) if k == DT else (k // 2, UNIT // k)

        def raw_half(u, h):
            k, n_ = half_shape(u)
            if k == DT:
                return view(u, DT)[:, :, h * P:(h + 1) * P]
            return ring[:, u % RING, h * HALF:(h + 1) * HALF].rearrange("p (k n) -> p k n", k=k)

        def split_half(part, u, h):
            return part[:, (2 * u + h) % SPLITS, :].rearrange("p (k n) -> p k n", k=half_shape(u)[0])

        LOADS_PER = 16 * (PER // RING)
        ROUTER_STEPS = 2 + 2 * TT + 1

        def split_hi(eng, x, i=None):
            u, h = x // 2, x % 2
            if h == 0:
                eng.wait_ge(loaded[u % RING], 16 * (u // RING + 1) + (0 if i is None else i * LOADS_PER))
            if x >= SPLITS:
                eng.wait_ge(half_done, x - SPLITS + 1 + (0 if i is None else i * 2 * PER))
            eng.activation(split_half(whi, u, h), raw_half(u, h), ACT.Copy).then_inc(hi_ready, 1)

        def split_lo(eng, x, i=None):
            u, h = x // 2, x % 2
            eng.wait_ge(hi_ready, x + 1 + (0 if i is None else i * 2 * PER))
            eng.tensor_tensor(split_half(wlo, u, h), raw_half(u, h), split_half(whi, u, h).bitcast(F32),
                              ALU.subtract).then_inc(lo_ready, 1)

        def run(eng, expert, last):
            with eng.Fori(0, NE) as i:
                expert(i, i)
            eng.wait_ge(over_ready, 1)
            more = eng.value_load(over[0:1, 0:1], min_val=0, max_val=1)
            with eng.If(more == 1):
                with eng.Fori(NE, 2 * NE) as i:
                    expert(i, i - NE)
                last(2)
            with eng.Else():
                last(1)

        block = ctx.enter_context(nc.Block())

        @block.sync
        def _(sp):
            sp.dma_start(resid[:, :, :], a["x"][0].rearrange("(t p) d -> p t d", p=P)).then_inc(x_loaded, 16)
            for name, (r, k) in rows.items():
                sp.dma_start(vrow[r:r + k, :], a[name][0].rearrange("(k p) -> k p", p=P)).then_inc(vectors_loaded, 16)
            sp.dma_start(vrow[SCW:NV, :], a["sc_conv_w"][0].rearrange("s (k p) -> (s k) p", p=P)).then_inc(vectors_loaded, 16)
            sp.dma_start(drow[0:ND, :], a["conv_dw_w"][0].rearrange("s (k p) -> (s k) p", p=P)).then_inc(vectors_loaded, 16)

            for u, (src, k, n_) in enumerate(units):
                if u >= RING:
                    sp.wait_ge(lo_ready, 2 * (u - RING + 1))
                sp.dma_start(view(u, k), src).then_inc(loaded[u % RING], 16)
                if u == 1:
                    for r in range(P // HD):
                        sp.dma_start(qkg[r * HD:(r + 1) * HD, 0:1], a["q_norm_g"].rearrange("a d -> d a")).then_inc(small_loaded, 16)
                        sp.dma_start(qkg[r * HD:(r + 1) * HD, 1:2], a["k_norm_g"].rearrange("a d -> d a")).then_inc(small_loaded, 16)
                    sp.dma_start(poolw, a["pool_w"][0].rearrange("g c d -> c g d")).then_inc(small_loaded, 16)
                    sp.dma_start(fb[:, :], a["forget_bias"].rearrange("a h -> h a")).then_inc(small_loaded, 16)
                    sp.dma_start(wf[:, :, :], od_in[:, 3 * C:3 * C + NH].rearrange("(k p) n -> p k n", p=P)).then_inc(small_loaded, 16)
                    sp.dma_start(wr[:, :, :], a["router_w"][0].rearrange("(k p) n -> p k n", p=P)).then_inc(small_loaded, 16)
                    sp.dma_start(rb[:, :], a["router_b"][0:1, :].to_broadcast([P, NE])).then_inc(small_loaded, 16)

            def load_expert(i, e, j):
                name, k0, c0 = expert_units[j]
                u = MOE + j
                if c0 is None:
                    src = a[name][0][e, k0 * P:(k0 + 2) * P, :].rearrange("(k p) n -> p k n", p=P)
                else:
                    src = a[name][0][e, k0 * P:(k0 + 4) * P, c0:c0 + 512].rearrange("(k p) n -> p k n", p=P)
                sp.wait_ge(lo_ready, i * (2 * PER) + 2 * (u - RING + 1))
                sp.dma_start(view(u, 2 if c0 is None else 4), src).then_inc(loaded[u % RING], 16)

            def expert(i, e):
                for j in range(PER):
                    load_expert(i, e, j)

            run(sp, expert, lambda rounds: sp.nop())
            sp.wait_ge(out_ready, 1)
            sp.dma_start(out[0].rearrange("(t p) d -> p t d", p=P), resid[:, :, :]).then_inc(out_stored, 16)
            sp.wait_ge(out_stored, 16)

        @block.gpsimd
        def _(pool):
            n = [0]

            def chain(ins):
                n[0] += 1
                ins.then_inc(pool_const, 1)
                pool.wait_ge(pool_const, n[0])

            chain(pool.memset(eps[:, :], EPS))
            chain(pool.memset(ident[:, :], 0.0))
            chain(pool.affine_select(out=ident[:, :], in_=ident[:, :], compare_op=ALU.not_equal, fill=1.0, base=0,
                                     pattern=[[-1, P]], channel_multiplier=1))
            chain(pool.iota(iota[:, :], pattern=[[1, T]], base=0, channel_multiplier=0,
                            allow_small_or_imprecise_dtypes=True))
            pool.memset(xpad, 0.0).then_inc(consts, 1)
            pool.memset(upad, 0.0).then_inc(consts, 1)
            pool.memset(ones[:, :], 1.0).then_inc(consts, 1)
            pool.memset(lnmean[:, :], 1.0 / C).then_inc(consts, 1)
            chain(pool.memset(before[:, :], 1.0))
            chain(pool.affine_select(out=before[:, :], in_=before[:, :], compare_op=ALU.is_gt, fill=0.0, base=0,
                                     pattern=[[1, P]], channel_multiplier=-1))
            chain(pool.memset(causal[:, :], 0.0))
            chain(pool.affine_select(out=causal[:, :], in_=causal[:, :], compare_op=ALU.is_ge, fill=NEG, base=0,
                                     pattern=[[-1, P]], channel_multiplier=1))
            chain(pool.memset(headmean[:, :], 0.0))
            for r in range(P // HD):
                pool.memset(headmean[r * HD:(r + 1) * HD, r * HD:(r + 1) * HD], 1.0 / HD).then_inc(consts, 1)
                pool.wait_ge(consts, 5 + r)

            m = [0]

            def step(ins):
                m[0] += 1
                ins.then_inc(pool_step, 1)
                pool.wait_ge(pool_step, m[0])

            L = PADP + T
            pool.wait_ge(u_ready, 2)
            pool.wait_ge(xpad_ready, 2)
            step(pool.tensor_tensor(winA[:, :, 1:L], xpad[:, :, 1:L], xpad[:, :, 0:L - 1], ALU.add))
            step(pool.tensor_tensor(winB[:, 1:, 3:L], winA[:, 1:, 3:L], winA[:, 1:, 1:L - 2], ALU.add))
            step(pool.tensor_tensor(winA[:, 2:, 7:L], winB[:, 2:, 7:L], winB[:, 2:, 3:L - 4], ALU.add))
            step(pool.tensor_tensor(winB[:, 3, 15:L], winA[:, 3, 15:L], winA[:, 3, 7:L - 8], ALU.add))
            pool.wait_ge(dve_const, 2 * CT)
            for g in range(CT):
                w = (winA if g % 2 == 0 else winB)[:, g, PADP:L]
                step(pool.tensor_tensor(w, w, rcount[:, g, :], ALU.mult))
                pool.tensor_tensor(w, w, xpad[:, g, PADP:L], ALU.subtract).then_inc(pooled_ready, 1)
                pool.wait_ge(pooled_ready, g + 1)

        @block.scalar
        def _(s):
            cursor = [0]

            def splits_to(n_):
                while cursor[0] < n_:
                    split_hi(s, cursor[0])
                    cursor[0] += 1

            def after_half(n_):
                splits_to(n_ + AHEAD)
                s.wait_ge(half_done, n_)

            def squares(k):
                for t in range(TT):
                    s.activation(normed[:, t, :], resid[:, t, :], ACT.Square, accum_out=ss[:, k, t:t + 1]).then_inc(sq_done, 1)
                s.wait_ge(sq_done, TT * (k + 1))
                s.activation(ss[:, k, :], ss[:, k, :], ACT.Sqrt, bias=eps[:, 0:1], scale=1.0 / D).then_inc(rms_ready, 1)

            def gain(k):
                for d in range(DT):
                    if d % 2 == 0:
                        s.wait_ge(turned, 4 * k + d // 2 + 1)
                    s.activation(xhi[:, d, :], bank[d // 2][:, (d % 2) * T:(d % 2 + 1) * T], ACT.Copy,
                                 scale=col(norms[k], d)).then_inc(xhi_ready, 1)

            s.wait_ge(pool_const, 1)
            s.wait_ge(x_loaded, 16)
            squares(0)
            splits_to(SPLITS)
            s.wait_ge(vec_ready, 2)
            gain(0)
            for j in range(2):
                after_half(2 * (E_IN + 2 * j + 2))
                s.activation(sig[:, j, :], bank[5 + 2 * j][:, :], ACT.Sigmoid).then_inc(sig_ready, 1)
            s.wait_ge(consts, 1)
            for j in range(2):
                after_half(2 * (E_IN + 5 + j))
                s.activation(xpad[:, 2 * j:2 * j + 2, PADP:], bank[j][:, :].rearrange("p (c t) -> p c t", c=2),
                             ACT.Copy).then_inc(xpad_ready, 1)
            splits_to(2 * E_OUT + SPLITS)
            for g in range(CT):
                s.wait_ge(poolmix_done, g // 2 + 1)
                s.activation(xhi[:, g, :], bank[2 + g // 2][:, (g % 2) * T:(g % 2 + 1) * T], ACT.Copy,
                             scale=col("pool_scale", g)).then_inc(xhi_ready, 1)
            splits_to(2 * E_OUT + 2 * SPLITS)
            for j in range(CT):
                s.wait_ge(xc_ready, j + 1)
                s.activation(csq[:, j, :], cacc[:, j, :], ACT.Square).then_inc(csq_ready, 1)
            s.wait_ge(cvar_done, 1)
            s.activation(crms[:, 0, :], bank[5][:, 0:T], ACT.Sqrt, bias=eps[:, 0:1]).then_inc(crms_ready, 1)
            for j in range(CT):
                s.wait_ge(cn_ready, j + 1)
                s.activation(csq[:, j, :], cacc[:, j, :], ACT.Silu, bias=col("conv_ln_b", j),
                             scale=col("conv_ln_g", j)).then_inc(cout_ready, 1)
                s.wait_ge(cout_ready, j + 1)
                s.activation(xhi[:, CT + j, :], csq[:, j, :], ACT.Copy).then_inc(xhi_ready, 1)
            XE = 2 * DT

            s.wait_ge(resid_ready, 4)
            squares(1)
            splits_to(2 * FFN + SPLITS)
            gain(1)
            for j in range(FB):
                after_half(2 * (ffn_gate[j] + 1))
                if j >= 2:
                    s.wait_ge(hid_ready, j - 1)
                s.activation(gated[:, j % 2, :], bank[4 + j % 2][:, :], ACT.Silu).then_inc(silu_ready, 1)
                splits_to(2 * (ffn_up[j] + 1) + AHEAD)
                s.wait_ge(hid_ready, j + 1)
                if j >= 2:
                    s.wait_ge(half_done, 2 * (ffn_down[j - 2] + 1))
                s.activation(hhi[:, j % 2, :], hidden[:, j % 2, :], ACT.Copy).then_inc(hhi_ready, 1)
            splits_to(2 * O_IN)
            s.wait_ge(resid_ready, 8)
            squares(2)
            splits_to(2 * O_IN + SPLITS)
            gain(2)
            s.wait_ge(f_step, 2)
            s.activation(fl[0:NH, 2, :], fl[0:NH, 1, :], ACT.Exp, scale=-1.0).then_inc(f_act, 1)
            s.wait_ge(f_act, 1)
            s.activation(fl[0:NH, 3, :], fl[0:NH, 2, :], ACT.Ln, bias=1.0).then_inc(f_act, 1)
            for m in range(4):
                after_half(2 * (O_Q + m + 1))
                s.activation(qsq[:, m, :], bank[4 + m][:, :], ACT.Square).then_inc(qsq_ready, 1)
            splits_to(2 * (O_V + 1))
            for m in range(4):
                s.wait_ge(qms_done, m + 1)
                s.activation(qsq[:, m, :], bank[2 + m % 2][:, :], ACT.Sqrt, bias=eps[:, 0:1]).then_inc(qrms_ready, 1)
                if m == 1:
                    splits_to(2 * (O_V + 1) + 2)
            after_half(2 * (O_V + 2))
            for t in range(TT):
                s.activation(v[:, t, :], bank[t][:, :], ACT.Copy).then_inc(v_ready, 1)
            for j in range(2):
                after_half(2 * (O_SX + j + 1))
                s.activation(sxs[:, 2 * j:2 * j + 2, :], bank[4 + j][:, :].rearrange("p (c t) -> p c t", c=2),
                             ACT.Copy).then_inc(sx_copied, 1)
            splits_to(2 * O_OUT + SPLITS)

            def attention_hi(i):
                h, q = i // 2, i % 2
                r = (h % 2) * HD
                s.wait_ge(o_done, i + 1)
                s.activation(xhi[r:r + HD, h // 2, q * P:(q + 1) * P], bank[2 + i % 2][r:r + HD, 0:P],
                             ACT.Copy).then_inc(o_hi, 1)

            def short_part(j):
                s.wait_ge(short_ready, j + 1)
                s.activation(xhi[:, CT + j, :], sacc[:, j, :], ACT.Copy).then_inc(short_hi, 1)

            for i in range(2 * NH + 2):
                if i < 2 * NH:
                    nk = (i % 2 + 1) * P
                    s.wait_ge(max_ready, i + 1)
                    s.activation(probs[:, i % 2, 0:nk], bank[4 + i % 2][:, 0:nk], ACT.Exp, bias=rmax[:, i, 1:2],
                                 accum_out=rmax[:, i, 2:3]).then_inc(exp_ready, 1)
                if i >= 2:
                    attention_hi(i - 2)
                if i >= STAPS * CT + 1 and i - STAPS * CT - 1 < CT:
                    short_part(i - STAPS * CT - 1)
            splits_to(2 * MOE)
            s.wait_ge(resid_ready, 12)
            s.dma_start(grow, a["od_norm_ffn"][0:1, :].to_broadcast([P, D])).then_inc(grow_loaded, 16)
            squares(3)
            for b in (2, 3):
                s.wait_ge(turned, 12 + b + 1)
                s.activation(hrT[:, 2 * b:2 * b + 2, :], bank[b][:, :].rearrange("p (c t) -> p c t", c=2),
                             ACT.Copy).then_inc(hr_hi, 1)
            s.wait_ge(r_step, ROUTER_STEPS)
            s.activation(lg[:, :, 10, 1], lg[:, :, 10, 0], ACT.Exp).then_inc(r_exp, 1)
            assert cursor[0] == 2 * MOE

            def gathered_hi(k):
                for h in range(2):
                    s.wait_ge(gathered, 2 * k + h + 1)
                    s.activation(xhi[:, 4 * h:4 * h + 4, 0:P], bank[(7, 1)[h]][:, :].rearrange("p (c t) -> p c t", c=4),
                                 ACT.Copy).then_inc(ehi_ready, 1)

            gathered_hi(0)

            def expert(i, e):
                mine = [2 * MOE]

                def more(n_):
                    while mine[0] < min(2 * MOE + n_, 2 * (MOE + PER)):
                        split_hi(s, mine[0], i)
                        mine[0] += 1

                def after(n_):
                    more(n_ + AHEAD)
                    s.wait_ge(half_done, i * (2 * PER) + 2 * MOE + n_)

                for c in range(EB + 1):
                    if c < EB:
                        after(2 * (moe_gate[c] + 2))
                        s.wait_ge(ehid_ready, 1 + i * EB + max(c - 1, 0))
                        s.activation(act[:, c % 2, :], bank[c % 2][:, :], ACT.Silu).then_inc(act_ready, 1)
                    if c >= 1:
                        if c == EB:
                            more(2 * (moe_down[c - 2] + 2) + AHEAD)
                        s.wait_ge(ehidT_done, 1 + i * EB + c)
                        s.activation(hhi[:, (c - 1) % 2, :], bank[6][:, :], ACT.Copy).then_inc(ehidT_hi, 1)
                gathered_hi(i + 1)
                after(2 * PER)
                s.activation(ye[:, 512:1024], bank[5][:, :], ACT.Copy).then_inc(ye_ready, 1)

            run(s, expert, lambda rounds: s.nop())

        @block.tensor
        def _(pe):
            def product(dst, lhs, rhs, start, stop):
                pe.matmul(dst, lhs[0], rhs[0], start=start, stop=False)
                pe.matmul(dst, lhs[0], rhs[1], start=False, stop=False)
                return pe.matmul(dst, lhs[1], rhs[0], start=False, stop=stop)

            def halves(u, i=None):
                for h in range(2):
                    x = 2 * u + h
                    pe.wait_ge(lo_ready, x + 1 + (0 if i is None else i * 2 * PER))
                    yield h, split_half(whi, u, h), split_half(wlo, u, h)

            def cols_product(u, b):
                for c, wh, wl in halves(u):
                    for k in range(DT):
                        mm = product(bank[b][:, c * T:(c + 1) * T], (wh[:, k, :], wl[:, k, :]),
                                     (xhi[:, k, :], xlo[:, k, :]), k == 0, k == DT - 1)
                    mm.then_inc(half_done, 1)

            def rows_product(u, lhs, first, last):
                for k, wh, wl in halves(u):
                    for t in range(TT):
                        for h in range(2):
                            cols = slice(h * 512, (h + 1) * 512)
                            mm = product(bank[2 * t + h][:, :], lhs(k, t), (wh[:, 0, cols], wl[:, 0, cols]),
                                         first and k == 0, last and k == 1)
                    mm.then_inc(half_done, 1)

            def turn(k):
                pe.wait_ge(normed_ready, TT * (k + 1 if k < 3 else 5))
                for b in range(4):
                    for c in range(2):
                        for t in range(TT):
                            d = 2 * b + c
                            mm = pe.transpose(bank[b][:, c * T + t * P:c * T + (t + 1) * P],
                                              normed[:, t, d * P:(d + 1) * P], ident[:, :])
                    mm.then_inc(turned, 1)

            def out_product(u0, ms):
                for m in ms:
                    rows_product(u0 + m, lambda k, t: tuple(x[:, 2 * m + k, t * P:(t + 1) * P] for x in (xhi, xlo)),
                                 m == 0, m == DT // 2 - 1)

            pe.wait_ge(pool_const, 3)
            pe.wait_ge(vectors_loaded, VECTORS)
            pe.transpose(bank[7][:, 0:NV], vrow[0:NV, :], ident[0:NV, 0:NV]).then_inc(vec_turned, 1)
            pe.transpose(bank[6][:, 0:ND], drow[0:ND, :], ident[0:ND, 0:ND]).then_inc(vec_turned, 1)
            turn(0)
            pe.wait_ge(xlo_ready, DT)
            pe.wait_ge(vec_ready, 2)
            for m, b in enumerate((4, 5, 6, 7, 0, 1)):
                cols_product(E_IN + m, b)
            pe.wait_ge(small_loaded, SMALL)
            for g in range(CT):
                pe.wait_ge(pooled_ready, g + 1)
                w = (winA if g % 2 == 0 else winB)[:, g, PADP:]
                mm = pe.matmul(bank[2 + g // 2][:, (g % 2) * T:(g % 2 + 1) * T], poolw[:, g, :], w, start=True, stop=True)
                if g % 2:
                    mm.then_inc(poolmix_done, 1)
            pe.wait_ge(xlo_ready, DT + CT)
            out_product(E_OUT, range(CT // 2))
            pe.wait_ge(conv_ready, 4)
            for j in range(CT):
                mm = pe.matmul(bank[4][:, 0:T], lnmean[:, :], cacc[:, j, :], start=(j == 0), stop=(j == CT - 1))
            mm.then_inc(mean_done, 1)
            for j in range(CT):
                pe.wait_ge(csq_ready, j + 1)
                mm = pe.matmul(bank[5][:, 0:T], lnmean[:, :], csq[:, j, :], start=(j == 0), stop=(j == CT - 1))
            mm.then_inc(cvar_done, 1)
            pe.wait_ge(xlo_ready, 2 * DT)
            out_product(E_OUT, range(CT // 2, DT // 2))

            pe.wait_ge(resid_ready, 4)
            turn(1)
            pe.wait_ge(xlo_ready, 3 * DT)
            for j in range(FB + 1):
                if j < FB:
                    if j >= 2:
                        pe.wait_ge(hid_ready, j - 1)
                    cols_product(ffn_gate[j], 4 + j % 2)
                    cols_product(ffn_up[j], 6 + j % 2)
                if j >= 1:
                    pe.wait_ge(hlo_ready, j)
                    rows_product(ffn_down[j - 1],
                                 lambda k, t: tuple(x[:, (j - 1) % 2, k * T + t * P:k * T + (t + 1) * P] for x in (hhi, hlo)),
                                 j == 1, j == FB)

            pe.wait_ge(resid_ready, 8)
            turn(2)
            pe.wait_ge(xlo_ready, 4 * DT)
            for k in range(DT):
                pe.matmul(bank[2][0:NH, 0:T], wf[:, k, :], xhi[:, k, :].bitcast(F32), start=(k == 0), stop=False)
                mm = pe.matmul(bank[2][0:NH, 0:T], wf[:, k, :], xlo[:, k, :].bitcast(F32), start=False, stop=(k == DT - 1))
            mm.then_inc(f_done, 1)
            for m in range(4):
                cols_product(O_Q + m, 4 + m)

            def head_means(m):
                pe.wait_ge(qsq_ready, m + 1)
                if m >= 2:
                    pe.wait_ge(qrms_ready, m - 1)
                pe.matmul(bank[2 + m % 2][:, :], headmean[:, :], qsq[:, m, :], start=True, stop=True).then_inc(qms_done, 1)

            pe.wait_ge(f_step, 1)
            head_means(0)
            head_means(1)
            for u in range(2):
                for h, wh, wl in halves(O_V + u):
                    for k in range(2):
                        for t in range(TT):
                            kk = 4 * u + 2 * h + k
                            mm = product(bank[t][:, :], tuple(x[:, kk, t * P:(t + 1) * P] for x in (xhi, xlo)),
                                         (wh[:, k, :], wl[:, k, :]), kk == 0, kk == DT - 1)
                    mm.then_inc(half_done, 1)
                if u == 0:
                    head_means(2)
                    head_means(3)
            for m, b in enumerate((4, 5, 6, 7, 0, 1)):
                if m < 4:
                    pe.wait_ge(qk_ready, m + 1)
                else:
                    pe.wait_ge(v_ready, TT)
                cols_product(O_SX + m, b)

            pe.wait_ge(f_ready, 2)
            pe.wait_ge(sx_copied, 2)
            pe.wait_ge(z_ready, 2)

            def scores(i):
                h, q = i // 2, i % 2
                nk, r = (q + 1) * P, (h % 2) * HD
                b = bank[4 + i % 2]
                if i >= 2:
                    pe.wait_ge(exp_ready, i - 1)
                qh = qkT[r:r + HD, h // 4, (h // 2) % 2, q * P:(q + 1) * P]
                kh = qkT[r:r + HD, 2 + h // 4, (h // 2) % 2, 0:nk]
                pick = ident[0:NH, h:h + 1]
                pe.matmul(b[:, 0:nk], qh, kh, start=True, stop=False)
                pe.matmul(b[:, nk - P:nk], ident[:, :], causal[:, :], start=False, stop=False)
                pe.matmul(b[:, 0:nk], fl[0:NH, 1, q * P:(q + 1) * P], pick.to_broadcast([NH, nk]), start=False, stop=False)
                pe.matmul(b[:, 0:nk], pick.to_broadcast([NH, P]), fl[0:NH, 2, 0:nk], start=False,
                          stop=True).then_inc(score_done, 1)

            def turn_probs(i):
                nk = (i % 2 + 1) * P
                pe.wait_ge(p_ready, i + 1)
                if i >= 2:
                    pe.wait_ge(pT_ready, i - 1)
                for c in range(nk // P):
                    mm = pe.transpose(bank[6 + i % 2][:, c * P:(c + 1) * P], probs[:, i % 2, c * P:(c + 1) * P], ident[:, :])
                mm.then_inc(pT_done, 1)

            def attend(i):
                h, q = i // 2, i % 2
                r = (h % 2) * HD
                pe.wait_ge(pT_ready, i + 1)
                if i >= 2:
                    pe.wait_ge(o_lo, i - 1)
                for c in range(q + 1):
                    mm = pe.matmul(bank[2 + i % 2][r:r + HD, 0:P], v[:, c, h * HD:(h + 1) * HD],
                                   probsT[:, i % 2, c * P:(c + 1) * P], start=(c == 0), stop=(c == q))
                mm.then_inc(o_done, 1)

            for i in range(2 * NH + 2):
                if i < 2 * NH:
                    scores(i)
                if 1 <= i <= 2 * NH:
                    turn_probs(i - 1)
                if i >= 2:
                    attend(i - 2)
            pe.wait_ge(o_lo, 2 * NH)
            pe.wait_ge(short_lo, CT)
            out_product(O_OUT, range(DT // 2))

            turn(3)
            pe.wait_ge(hr_lo, 2)
            pe.wait_ge(hr_hi, 2)
            for t in range(TT):
                for k in range(DT):
                    mm = pe.matmul(bank[4 + t][:, 0:NE], hrT[:, k, t * P:(t + 1) * P], wr[:, k, :],
                                   start=(k == 0), stop=(k == DT - 1))
                mm.then_inc(logits_done, 1)
            pe.wait_ge(mask_ready, 1)
            pe.matmul(bank[6][:, 0:NE], before[:, :], lg[:, 0, 8, :], start=True, stop=True).then_inc(count_done, 1)
            pe.matmul(bank[7][:, 0:NE], ones[:, 0:P], lg[:, 0, 8, :], start=True, stop=False)
            pe.matmul(bank[7][:, 0:NE], before[:, :], lg[:, 1, 8, :], start=False, stop=True).then_inc(count_done, 1)
            pe.matmul(bank[5][:, 0:NE], ones[:, 0:P], lg[:, 0, 8, :], start=True, stop=False)
            pe.matmul(bank[5][:, 0:NE], ones[:, 0:P], lg[:, 1, 8, :], start=False, stop=True).then_inc(count_done, 1)

            def gather(k):
                pe.wait_ge(disp_ready, 4 * k + 4)
                for h in range(2):
                    for c in range(4):
                        for t in range(TT):
                            d = 4 * h + c
                            mm = pe.matmul(bank[(7, 1)[h]][:, c * P:(c + 1) * P], normed[:, t, d * P:(d + 1) * P],
                                           disp[:, t, :], start=(t == 0), stop=(t == TT - 1))
                    mm.then_inc(gathered, 1)

            gather(0)
            for free in (dispT_done, ehidT_done):
                pe.sem_inc(free, 1)

            def expert(i, e):
                def up_product(j, b):
                    for g in range(2):
                        for h, wh, wl in halves(MOE + j + g, i):
                            for k in range(2):
                                kk = 4 * g + 2 * h + k
                                mm = product(bank[b][:, :], (xhi[:, kk, 0:P], xlo[:, kk, 0:P]),
                                             (wh[:, k, :], wl[:, k, :]), kk == 0, kk == DT - 1)
                            mm.then_inc(half_done, 1)

                pe.wait_ge(elo_ready, i * 2 + 2)
                for c in range(EB + 1):
                    if c < EB:
                        pe.wait_ge(ehid_ready, 1 + i * EB + max(c - 1, 0))
                        if c == 1:
                            pe.wait_ge(added, 1 + i * 4)
                        up_product(moe_gate[c], c % 2)
                    if c == 1:
                        for t in range(TT):
                            mm = pe.transpose(bank[7][:, t * P:(t + 1) * P], dispw[:, t, :], ident[:, :])
                        mm.then_inc(dispT_done, 1)
                    if c >= 1:
                        pe.wait_ge(ehid_ready, 1 + i * EB + c)
                        pe.wait_ge(ehidT_lo, 1 + i * EB + c - 1)
                        for f in range(4):
                            mm = pe.transpose(bank[6][:, f * P:(f + 1) * P], ehid[:, (c - 1) % 2, f * P:(f + 1) * P],
                                              ident[:, :])
                        mm.then_inc(ehidT_done, 1)
                    if c == EB:
                        pe.wait_ge(dispT_ready, i + 1)
                        gather(i + 1)
                    if c < EB:
                        up_product(moe_up[c], 2 + c % 2)
                    if c >= 1:
                        pe.wait_ge(ehidT_lo, 1 + i * EB + c)
                        if c == 1:
                            pe.wait_ge(ye_ready, 1 + i * 2)
                        for g in range(2):
                            for h, wh, wl in halves(MOE + moe_down[c - 1] + g, i):
                                for n_ in range(2):
                                    cols = slice(n_ * 512, (n_ + 1) * 512)
                                    f = (2 * g + h) * P
                                    mm = product(bank[4 + n_][:, :],
                                                 tuple(x[:, (c - 1) % 2, f:f + P] for x in (hhi, hlo)),
                                                 (wh[:, 0, cols], wl[:, 0, cols]), c == 1 and g == 0 and h == 0,
                                                 c == EB and g == 1 and h == 1)
                                mm.then_inc(half_done, 1)
                pe.wait_ge(ye_ready, 1 + i * 2 + 2)
                pe.wait_ge(elo_ready, i * 2 + 4)
                for t in range(TT):
                    for h in range(2):
                        pe.matmul(bank[(1, 3, 6, 7)[2 * t + h]][:, :], dispT[:, t, :], ye[:, h * 512:(h + 1) * 512],
                                  start=True, stop=True).then_inc(scattered, 1)

            run(pe, expert, lambda rounds: pe.nop())

        @block.vector
        def _(d):
            cursor = [0]

            def splits_to(n_):
                while cursor[0] < n_:
                    split_lo(d, cursor[0])
                    cursor[0] += 1

            def after_half(n_):
                splits_to(n_ + AHEAD)
                d.wait_ge(half_done, n_)

            for g, w in enumerate(WINDOWS):
                if g == 0:
                    d.wait_ge(pool_const, 4)
                d.tensor_scalar(rcount[:, g, :], iota[:, :], 1.0, float(w), ALU.add, ALU.min).then_inc(dve_const, 1)
            for g in range(CT):
                d.wait_ge(dve_const, g + 1)
                d.reciprocal(rcount[:, g, :], rcount[:, g, :]).then_inc(dve_const, 1)
            d.wait_ge(vec_turned, 2)
            d.tensor_copy(vcol[:, 0:NV], bank[7][:, 0:NV]).then_inc(vec_ready, 1)
            d.tensor_copy(dcol[:, 0:ND], bank[6][:, 0:ND]).then_inc(vec_ready, 1)

            def normalize(k):
                d.wait_ge(rms_ready, k + 1)
                d.reciprocal(rstd[:, k, :], ss[:, k, :]).then_inc(rstd_ready, 1)
                d.wait_ge(rstd_ready, k + 1)
                for t in range(TT):
                    d.tensor_scalar(normed[:, t, :], resid[:, t, :], rstd[:, k, t:t + 1], None, ALU.mult).then_inc(normed_ready, 1)

            def scaled_lo(dst, src, scale, hi):
                return d.scalar_tensor_tensor(out=dst, in0=src, scalar=scale, in1=hi.bitcast(F32), op0=ALU.mult,
                                              op1=ALU.subtract)

            def gain(k):
                for n_ in range(DT):
                    if n_ % 2 == 0:
                        d.wait_ge(xhi_ready, DT * (k if k == 0 else k + 1) + n_ + 2)
                    scaled_lo(xlo[:, n_, :], bank[n_ // 2][:, (n_ % 2) * T:(n_ % 2 + 1) * T], col(norms[k], n_),
                              xhi[:, n_, :]).then_inc(xlo_ready, 1)

            def residual(u):
                splits_to(2 * u)
                d.wait_ge(half_done, 2 * u)
                for t in range(TT):
                    for h in range(2):
                        r = resid[:, t, h * 512:(h + 1) * 512]
                        d.tensor_tensor(r, r, bank[2 * t + h][:, :], ALU.add).then_inc(resid_ready, 1)

            d.wait_ge(x_loaded, 16)
            normalize(0)
            splits_to(SPLITS)
            d.wait_ge(vec_ready, 2)
            gain(0)
            d.wait_ge(consts, 2)
            for j in range(2):
                splits_to(2 * (E_IN + 2 * j + 2) + AHEAD)
                d.wait_ge(sig_ready, j + 1)
                d.tensor_tensor(upad[:, 2 * j:2 * j + 2, PADC:], bank[4 + 2 * j][:, :].rearrange("p (c t) -> p c t", c=2),
                                sig[:, j, :].rearrange("p (c t) -> p c t", c=2), ALU.mult).then_inc(u_ready, 1)
            splits_to(2 * E_OUT)
            for s_ in range(TAPS):
                if s_ == 8:
                    splits_to(2 * E_OUT + SPLITS)
                if s_ == 20:
                    for g in range(CT):
                        d.wait_ge(xhi_ready, DT + (g // 2) * 2 + 2)
                        scaled_lo(xlo[:, g, :], bank[2 + g // 2][:, (g % 2) * T:(g % 2 + 1) * T], col("pool_scale", g),
                                  xhi[:, g, :]).then_inc(xlo_ready, 1)
                for j in range(CT):
                    w = dcol[:, s_ * CT + j:s_ * CT + j + 1]
                    src = upad[:, j, s_:s_ + T]
                    if s_ == 0:
                        d.wait_ge(u_ready, j // 2 + 1)
                        ins = d.tensor_scalar(cacc[:, j, :], src, w, col("conv_dw_b", j), ALU.mult, ALU.add)
                    else:
                        d.wait_ge(conv_step, (s_ - 1) * CT + j + 1)
                        ins = d.scalar_tensor_tensor(out=cacc[:, j, :], in0=src, scalar=w, in1=cacc[:, j, :],
                                                     op0=ALU.mult, op1=ALU.add)
                    ins.then_inc(conv_ready if s_ == TAPS - 1 else conv_step, 1)
            splits_to(2 * E_OUT + 2 * SPLITS)
            d.wait_ge(mean_done, 1)
            for j in range(CT):
                d.wait_ge(conv_ready, j + 1)
                d.tensor_tensor(cacc[:, j, :], cacc[:, j, :], bank[4][:, 0:T], ALU.subtract).then_inc(xc_ready, 1)
            d.wait_ge(crms_ready, 1)
            d.reciprocal(crms[:, 1, :], crms[:, 0, :]).then_inc(crstd_ready, 1)
            d.wait_ge(crstd_ready, 1)
            for j in range(CT):
                d.wait_ge(xc_ready, j + 1)
                d.wait_ge(csq_ready, j + 1)
                d.tensor_tensor(cacc[:, j, :], cacc[:, j, :], crms[:, 1, :], ALU.mult).then_inc(cn_ready, 1)
            for j in range(CT):
                d.wait_ge(xhi_ready, DT + CT + j + 1)
                d.tensor_tensor(xlo[:, CT + j, :], csq[:, j, :], xhi[:, CT + j, :].bitcast(F32), ALU.subtract).then_inc(xlo_ready, 1)

            residual(FFN)
            normalize(1)
            splits_to(2 * FFN + SPLITS)
            gain(1)
            for j in range(FB):
                splits_to(2 * (ffn_gate[j] + 1) + AHEAD)
                after_half(2 * (ffn_up[j] + 1))
                d.wait_ge(silu_ready, j + 1)
                if j >= 2:
                    d.wait_ge(hhi_ready, j - 1)
                d.tensor_tensor(hidden[:, j % 2, :], gated[:, j % 2, :], bank[6 + j % 2][:, :], ALU.mult).then_inc(hid_ready, 1)
                if j >= 2:
                    d.wait_ge(half_done, 2 * (ffn_down[j - 2] + 1))
                d.wait_ge(hhi_ready, j + 1)
                d.tensor_tensor(hlo[:, j % 2, :], hidden[:, j % 2, :], hhi[:, j % 2, :].bitcast(F32),
                                ALU.subtract).then_inc(hlo_ready, 1)
            residual(O_IN)
            normalize(2)
            splits_to(2 * O_IN + SPLITS)
            gain(2)
            z, az, lse, F_, negF = (fl[0:NH, k, :] for k in (0, 1, 3, 1, 2))
            d.wait_ge(f_done, 1)
            d.wait_ge(small_loaded, SMALL)
            d.tensor_scalar(z, bank[2][0:NH, 0:T], fb[:, 0:1], None, ALU.add).then_inc(f_step, 1)
            d.wait_ge(f_step, 1)
            d.scalar_tensor_tensor(out=az, in0=z, scalar=-1.0, in1=z, op0=ALU.mult, op1=ALU.max).then_inc(f_step, 1)
            d.wait_ge(f_act, 2)
            d.scalar_tensor_tensor(out=z, in0=z, scalar=0.0, in1=lse, op0=ALU.min, op1=ALU.subtract).then_inc(f_step, 1)
            d.wait_ge(f_step, 3)
            d.tensor_tensor_scan(F_, ones[0:NH, :], z, 0.0, ALU.mult, ALU.add).then_inc(f_ready, 1)
            d.wait_ge(f_ready, 1)
            d.tensor_scalar(negF, F_, -1.0, None, ALU.mult).then_inc(f_ready, 1)
            d.tensor_scalar(qkg[:, 0:1], qkg[:, 0:1], float(HD) ** -0.5, None, ALU.mult).then_inc(f_ready, 1)
            d.wait_ge(f_ready, 3)
            splits_to(2 * (O_V + 1))
            for m in range(4):
                if m == 2:
                    splits_to(2 * (O_V + 1) + 2)
                d.wait_ge(qrms_ready, m + 1)
                d.reciprocal(qsq[:, m, :], qsq[:, m, :]).then_inc(qrstd_ready, 1)
                d.wait_ge(qrstd_ready, m + 1)
                d.scalar_tensor_tensor(out=qkT[:, m, :, :].rearrange("p c t -> p (c t)"), in0=bank[4 + m][:, :],
                                       scalar=qkg[:, m // 2:m // 2 + 1], in1=qsq[:, m, :], op0=ALU.mult,
                                       op1=ALU.mult).then_inc(qk_ready, 1)
            d.memset(spad[:, :, 0:PADS], 0.0).then_inc(z_ready, 1)
            for j in range(2):
                after_half(2 * (O_SC + j + 1))
                d.wait_ge(sx_copied, j + 1)
                d.tensor_tensor(spad[:, 2 * j:2 * j + 2, PADS:], bank[6 + j][:, :].rearrange("p (c t) -> p c t", c=2),
                                sxs[:, 2 * j:2 * j + 2, :], ALU.mult).then_inc(z_ready, 1)
            splits_to(2 * O_OUT + SPLITS)
            short = [(s_, j) for s_ in range(STAPS) for j in range(CT)]

            def short_tap(s_, j):
                w = vcol[:, SCW + s_ * CT + j:SCW + s_ * CT + j + 1]
                src = spad[:, j, s_:s_ + T]
                if s_ == 0:
                    d.wait_ge(z_ready, j // 2 + 2)
                    ins = d.tensor_scalar(sacc[:, j, :], src, w, None, ALU.mult)
                else:
                    d.wait_ge(s_step, (s_ - 1) * CT + j + 1)
                    ins = d.scalar_tensor_tensor(out=sacc[:, j, :], in0=src, scalar=w, in1=sacc[:, j, :],
                                                 op0=ALU.mult, op1=ALU.add)
                ins.then_inc(s_step, 1)

            def short_gate(j):
                d.wait_ge(half_done, 2 * (O_SB + 2))
                d.wait_ge(s_step, (STAPS - 1) * CT + j + 1)
                d.tensor_tensor(sacc[:, j, :], sacc[:, j, :], bank[j // 2][:, (j % 2) * T:(j % 2 + 1) * T],
                                ALU.mult).then_inc(short_ready, 1)

            def short_rest(j):
                d.wait_ge(short_hi, j + 1)
                d.tensor_tensor(xlo[:, CT + j, :], sacc[:, j, :], xhi[:, CT + j, :].bitcast(F32),
                                ALU.subtract).then_inc(short_lo, 1)

            def softmax_max(i):
                nk = (i % 2 + 1) * P
                d.wait_ge(score_done, i + 1)
                d.tensor_reduce(rmax[:, i, 0:1], bank[4 + i % 2][:, 0:nk], AX.X, ALU.max).then_inc(max_step, 1)
                d.wait_ge(max_step, i + 1)
                d.tensor_scalar(rmax[:, i, 1:2], rmax[:, i, 0:1], -1.0, None, ALU.mult).then_inc(max_ready, 1)

            def softmax_norm(i):
                nk = (i % 2 + 1) * P
                d.wait_ge(exp_ready, i + 1)
                d.reciprocal(rmax[:, i, 3:4], rmax[:, i, 2:3]).then_inc(p_step, 1)
                d.wait_ge(p_step, i + 1)
                d.tensor_scalar(probs[:, i % 2, 0:nk], probs[:, i % 2, 0:nk], rmax[:, i, 3:4], None,
                                ALU.mult).then_inc(p_ready, 1)

            def copy_pT(i):
                nk = (i % 2 + 1) * P
                d.wait_ge(pT_done, i + 1)
                d.tensor_copy(probsT[:, i % 2, 0:nk], bank[6 + i % 2][:, 0:nk]).then_inc(pT_ready, 1)

            def attention_lo(i):
                h, q = i // 2, i % 2
                r = (h % 2) * HD
                d.wait_ge(o_hi, i + 1)
                d.tensor_tensor(xlo[r:r + HD, h // 2, q * P:(q + 1) * P], bank[2 + i % 2][r:r + HD, 0:P],
                                xhi[r:r + HD, h // 2, q * P:(q + 1) * P].bitcast(F32), ALU.subtract).then_inc(o_lo, 1)

            for i in range(2 * NH + 2):
                if i < 2 * NH:
                    softmax_max(i)
                if i < len(short):
                    short_tap(*short[i])
                elif i < len(short) + CT:
                    short_gate(i - len(short))
                if i < 2 * NH:
                    softmax_norm(i)
                if 1 <= i <= 2 * NH:
                    copy_pT(i - 1)
                if i >= 2:
                    attention_lo(i - 2)
            for j in range(CT):
                short_rest(j)
            residual(MOE)
            assert cursor[0] == 2 * MOE
            normalize(3)
            d.wait_ge(grow_loaded, 16)
            for t in range(TT):
                d.wait_ge(normed_ready, 6 + t + 1)
                d.tensor_tensor(normed[:, t, :], normed[:, t, :], grow, ALU.mult).then_inc(normed_ready, 1)
            for b in (0, 1):
                d.wait_ge(turned, 12 + b + 1)
                d.tensor_copy(hrT[:, 2 * b:2 * b + 2, :], bank[b][:, :].rearrange("p (c t) -> p c t", c=2)).then_inc(hr_lo, 1)

            r = [0]

            def chain(ins):
                r[0] += 1
                ins.then_inc(r_step, 1)
                d.wait_ge(r_step, r[0])

            chain(d.memset(pos[:, :, 2 * NE:], -1.0))
            chain(d.memset(comb[:, :, 2 * NE:], 0.0))
            d.wait_ge(logits_done, TT)
            for t in range(TT):
                chain(d.tensor_tensor(lg[:, t, 0, :], bank[4 + t][:, 0:NE], rb[:, :], ALU.add))
            for t in range(TT):
                chain(d.max(lg[:, t, 1, :], lg[:, t, 0, :]))
            chain(d.tensor_tensor(lg[:, :, 10, 0], lg[:, :, 1, 1], lg[:, :, 1, 0], ALU.subtract))
            assert r[0] == ROUTER_STEPS
            for t in range(TT):
                chain(d.max_index(idx[:, t, :], lg[:, t, 1, :], lg[:, t, 0, :]))
            chain(d.tensor_copy(lg[:, :, 2, 0:2], idx[:, :, 0:2]))
            for t in range(TT):
                for k in range(2):
                    chain(d.tensor_scalar(lg[:, t, 3 + k, :], iota[:, 0:NE], lg[:, t, 2, k:k + 1], None, ALU.is_equal))
            d.tensor_tensor(lg[:, :, 8, :], lg[:, :, 3, :], lg[:, :, 4, :], ALU.add).then_inc(mask_ready, 1)
            d.wait_ge(r_exp, 1)
            chain(d.tensor_scalar(lg[:, :, 10, 2], lg[:, :, 10, 1], 1.0, None, ALU.add))
            chain(d.reciprocal(lg[:, :, 10, 3], lg[:, :, 10, 2]))
            chain(d.tensor_tensor(lg[:, :, 10, 4], lg[:, :, 10, 3], lg[:, :, 10, 1], ALU.mult))
            for t in range(TT):
                chain(d.tensor_scalar(lg[:, t, 5, :], lg[:, t, 3, :], lg[:, t, 10, 3:4], None, ALU.mult))
                chain(d.scalar_tensor_tensor(out=comb[:, t, 0:NE], in0=lg[:, t, 4, :], scalar=lg[:, t, 10, 4:5],
                                             in1=lg[:, t, 5, :], op0=ALU.mult, op1=ALU.add))
            chain(d.tensor_copy(comb[:, :, NE:2 * NE], comb[:, :, 0:NE]))
            d.wait_ge(count_done, 3)
            d.wait_ge(mask_ready, 1)
            for t in range(TT):
                chain(d.scalar_tensor_tensor(out=lg[:, t, 6, :], in0=bank[6 + t][:, 0:NE], scalar=1.0,
                                             in1=lg[:, t, 8, :], op0=ALU.add, op1=ALU.mult))
            chain(d.tensor_scalar(pos[:, :, 0:NE], lg[:, :, 6, :], -1.0, None, ALU.add))
            chain(d.tensor_scalar(pos[:, :, NE:2 * NE], lg[:, :, 6, :], -1.0 - P, None, ALU.add))

            def dispatch(k):
                for t in range(TT):
                    where = pos[:, t, bass.ds(k, 1)]
                    d.tensor_scalar(disp[:, t, :], iota[:, 0:P], where, None, ALU.is_equal).then_inc(disp_ready, 1)
                    d.tensor_scalar(dispw[:, t, :], iota[:, 0:P], where, comb[:, t, bass.ds(k, 1)], ALU.is_equal,
                                    ALU.mult).then_inc(disp_ready, 1)

            def gathered_lo(k):
                for h in range(2):
                    d.wait_ge(ehi_ready, 2 * k + h + 1)
                    d.tensor_tensor(xlo[:, 4 * h:4 * h + 4, 0:P], bank[(7, 1)[h]][:, :].rearrange("p (c t) -> p c t", c=4),
                                    xhi[:, 4 * h:4 * h + 4, 0:P].bitcast(F32), ALU.subtract).then_inc(elo_ready, 1)

            dispatch(0)
            chain(d.tensor_reduce(cnt[:, 0:1], bank[5][:, 0:NE], AX.X, ALU.max))
            chain(d.tensor_scalar(cnt[:, 1:2], cnt[:, 0:1], float(P), None, ALU.is_gt))
            d.tensor_copy(over[:, :], cnt[:, 1:2]).then_inc(over_ready, 1)
            gathered_lo(0)
            for free in (added, ehid_ready, ehidT_lo, ye_ready):
                d.sem_inc(free, 1)

            def expert(i, e):
                mine = [2 * MOE]

                def more(n_):
                    while mine[0] < min(2 * MOE + n_, 2 * (MOE + PER)):
                        split_lo(d, mine[0], i)
                        mine[0] += 1

                def after(n_):
                    more(n_ + AHEAD)
                    d.wait_ge(half_done, i * (2 * PER) + 2 * MOE + n_)

                for c in range(EB + 1):
                    more(2 * ((moe_gate[c] if c < EB else moe_down[c - 2]) + 2) + AHEAD)
                    if c == 2:
                        d.wait_ge(dispT_done, 1 + i + 1)
                        d.tensor_copy(dispT, bank[7][:, 0:TT * P].rearrange("p (t s) -> p t s", t=TT)).then_inc(dispT_ready, 1)
                    if c == 4:
                        dispatch(i + 1)
                    if c >= 1:
                        d.wait_ge(ehidT_hi, i * EB + c)
                        d.tensor_tensor(hlo[:, (c - 1) % 2, :], bank[6][:, :], hhi[:, (c - 1) % 2, :].bitcast(F32),
                                        ALU.subtract).then_inc(ehidT_lo, 1)
                    if c < EB:
                        after(2 * (moe_up[c] + 2))
                        d.wait_ge(act_ready, i * EB + c + 1)
                        d.wait_ge(ehidT_done, 1 + i * EB + max(c - 1, 0))
                        d.tensor_tensor(ehid[:, c % 2, :], act[:, c % 2, :], bank[2 + c % 2][:, :], ALU.mult).then_inc(ehid_ready, 1)
                gathered_lo(i + 1)
                after(2 * PER)
                d.tensor_copy(ye[:, 0:512], bank[4][:, :]).then_inc(ye_ready, 1)
                for t in range(TT):
                    for h in range(2):
                        d.wait_ge(scattered, i * 4 + 2 * t + h + 1)
                        r_ = resid[:, t, h * 512:(h + 1) * 512]
                        d.tensor_tensor(r_, r_, bank[(1, 3, 6, 7)[2 * t + h]][:, :], ALU.add).then_inc(added, 1)

            def finish(rounds):
                d.wait_ge(added, 1 + 4 * NE * rounds)
                d.tensor_copy(cnt[:, 0:1], cnt[:, 1:2]).then_inc(out_ready, 1)

            run(d, expert, finish)


def kernel(**inputs):
    import numpy as np
    import concourse.bacc as bacc
    from concourse.bass_utils import run_bass_kernel_spmd

    nc = bacc.Bacc("TRN2", target_bir_lowering=False, num_devices=1,
                   dynamic_dma_scratch_size=1024)
    arrays, args = {}, {}
    for name, value in inputs.items():
        value = np.ascontiguousarray(value)
        arrays[f"in_{name}"] = value
        args[name] = nc.dram_tensor(f"in_{name}", value.shape, mybir.dt.from_np(value.dtype), kind="ExternalInput").ap()
    shape = inputs["x"].shape
    result = nc.dram_tensor("out_x", shape, F32, kind="ExternalOutput").ap()
    build_trunk(nc, args, result)
    ran = run_bass_kernel_spmd(nc, [arrays], core_ids=[0])
    return ran.results[0]["out_x"]
```

```python
from contextlib import ExitStack

import concourse.bass as bass
from concourse import mybir

F32 = mybir.dt.float32
F32R = mybir.dt.float32r
I32 = mybir.dt.int32
ALU = mybir.AluOpType
ACT = mybir.ActivationFunctionType
AX = mybir.AxisListType

P = 128
UNIT = 2048
RING = 14
HALF = UNIT // 2
SPLITS = 4
AHEAD = 3
EPS = 1e-6
WINDOWS = (2, 4, 8, 16)
NEG = -1.0e30


def build_trunk(nc, a, out):
    T, D = a["x"].shape[1:]
    TT, DT = T // P, D // P
    C = a["pool_scale"].shape[1]
    CT = C // P
    TAPS = a["conv_dw_w"].shape[1]
    STAPS = a["sc_conv_w"].shape[1]
    F = a["ffn_w_gate"].shape[2]
    NH = a["forget_bias"].shape[1]
    HD = a["q_norm_g"].shape[1]
    NE = a["router_w"].shape[2]
    FE = a["moe_w_gate"].shape[3]
    PADC, PADS, PADP = TAPS - 1, STAPS - 1, max(WINDOWS) - 1
    FB = F // 256
    EB = FE // 512

    def cols_unit(w, c0):
        return w[:, c0:c0 + 256].rearrange("(k p) n -> p k n", p=P), DT, 256

    def half_unit(w, k0, c0):
        return w[k0 * P:(k0 + 4) * P, c0:c0 + 512].rearrange("(k p) n -> p k n", p=P), 4, 512

    def rows_unit(w, k0):
        return w[k0 * P:(k0 + 2) * P, :].rearrange("(k p) n -> p k n", p=P), 2, D

    ev_in, od_in = a["ev_w_in"][0], a["od_w_in"][0]
    wg, wu, wd = a["ffn_w_gate"][0], a["ffn_w_up"][0], a["ffn_w_down"][0]
    units = [cols_unit(ev_in, c) for c in (C, 2 * C, C + 256, 2 * C + 256, 0, 256)]
    E_IN = 0
    E_OUT = len(units)
    units += [rows_unit(a["ev_w_out"][0], 2 * m) for m in range(DT // 2)]
    FFN = len(units)
    ffn_gate, ffn_up, ffn_down = {}, {}, {}
    for j in range(FB + 1):
        if j < FB:
            ffn_gate[j] = len(units)
            units.append(cols_unit(wg, 256 * j))
            ffn_up[j] = len(units)
            units.append(cols_unit(wu, 256 * j))
        if j >= 1:
            ffn_down[j - 1] = len(units)
            units.append(rows_unit(wd, 2 * (j - 1)))
    O_IN = len(units)
    S0 = 3 * C + NH
    units += [cols_unit(od_in, c) for c in (0, 256, C, C + 256)]
    units += [half_unit(od_in, k, 2 * C) for k in (0, 4)]
    units += [cols_unit(od_in, S0 + c) for c in (0, 256, 2 * C, 2 * C + 256, C, C + 256)]
    O_Q, O_K, O_V, O_SX, O_SC, O_SB = O_IN, O_IN + 2, O_IN + 4, O_IN + 6, O_IN + 8, O_IN + 10
    O_OUT = len(units)
    units += [rows_unit(a["od_w_out"][0], 2 * m) for m in range(DT // 2)]
    MOE = len(units)
    moe_gate, moe_up, moe_down, PER = {}, {}, {}, 0
    expert_units = []
    for c in range(EB + 1):
        if c < EB:
            moe_gate[c], moe_up[c] = PER, PER + 2
            expert_units += [("moe_w_gate", 4 * h, 512 * c) for h in (0, 1)]
            expert_units += [("moe_w_up", 4 * h, 512 * c) for h in (0, 1)]
            PER += 4
        if c >= 1:
            moe_down[c - 1] = PER
            expert_units += [("moe_w_down", 4 * (c - 1) + 2 * h, None) for h in (0, 1)]
            PER += 2
    assert PER == len(expert_units) and PER % RING == 0

    with ExitStack() as ctx:
        def sb(name, shape, dt=F32):
            return ctx.enter_context(nc.sbuf_tensor(name, shape, dt))

        def sem(name):
            return ctx.enter_context(nc.semaphore(name))

        FR = 64 + NH
        HR = 32 + 2 * NH
        ring = sb("ring", [P, RING, UNIT])
        whi = sb("whi", [P, SPLITS, HALF], F32R)
        wlo = sb("wlo", [P, SPLITS, HALF], F32R)
        resid = sb("resid", [P, TT, D])
        normed = sb("normed", [P, TT, D])
        xhi = sb("xhi", [P, DT, T], F32R)
        xlo = sb("xlo", [P, DT, T], F32R)
        hhi = sb("hhi", [P, 2, 512], F32R)
        hlo = sb("hlo", [P, 2, 512], F32R)
        ohi = hhi[:, :, :].rearrange("p a (b t) -> p (a b) t", t=T)
        olo = hlo[:, :, :].rearrange("p a (b t) -> p (a b) t", t=T)
        wfhi = hlo[:, :, :].rearrange("p a b -> p (a b)")[:, 0:DT * FR].rearrange("p (k r) -> p k r", r=FR)
        wflo = sb("wflo", [P, DT, FR], F32R)
        heads = hhi[0:HR, :, :].rearrange("p a b -> p (a b)")

        split_rows = sb("split_rows", [P, 2, T], F32R)
        fsum = split_rows[0:FR, 0, :]
        fneg = split_rows[0:FR, 1, :]
        dispT = split_rows[:, 0, :].rearrange("p (t s) -> p t s", t=TT)
        rqT = hlo[0:HR, :, :].rearrange("p a b -> p (a b)")[:, DT * FR:DT * FR + T]
        yhi, ylo = (x[:, :, P:T].rearrange("p (h c) n -> p h c n", h=2) for x in (xhi, xlo))

        PTAPS, DIAGS = 10, 8
        VTAPS = TAPS - PTAPS
        UW = T + PTAPS - 1
        diag_hi, diag_lo = (x[:, :, :].rearrange("p a b -> p (a b)").rearrange("p (g n) -> p g n", n=P) for x in (hhi, hlo))

        def u_part(lo, j):
            if j < 3:
                return (xlo if lo else xhi)[:, CT:, :].rearrange("p c t -> p (c t)")[:, j * UW:(j + 1) * UW]
            return wflo[:, :, :].rearrange("p k r -> p (k r)")[:, lo * UW:(lo + 1) * UW]

        ARENA = 6152
        arena = sb("arena", [P, ARENA])

        class Phase:
            def __init__(self):
                self.at = 0

            def take(self, *dims):
                n = 1
                for x in dims:
                    n *= x
                flat = arena[:, self.at:self.at + n]
                self.at += n
                assert self.at <= ARENA
                if len(dims) == 1:
                    return flat
                if len(dims) == 2:
                    return flat.rearrange("p (a b) -> p a b", a=dims[0])
                return flat.rearrange("p (a b c) -> p a b c", a=dims[0], b=dims[1])

        even = Phase()
        upad = even.take(CT, PADC + T)
        cacc = even.take(CT, T)
        xpad = normed[:, :, :].rearrange("p t d -> p (t d)")[:, 0:CT * (PADP + T)].rearrange("p (c t) -> p c t", c=CT)
        winA = even.take(CT, PADP + T)
        winB = even.take(CT, PADP + T)
        rcount = even.take(CT, T)
        poolw = even.take(CT, P)
        ctmp = even.take(T)
        csq = rcount
        crms = xpad[:, 0:2, 0:T]
        sig = winA.rearrange("p a b -> p (a b)")[:, 0:1024].rearrange("p (a b) -> p a b", a=2)
        ffn = Phase()
        gated = ffn.take(2, 512)
        hidden = ffn.take(2, 512)
        odd = Phase()
        qkT = odd.take(4, 2, T)
        qsq = normed[:, :, :].rearrange("p t (m n) -> p (t m) n", n=512)
        v = odd.take(TT, C)
        fl = odd.take(4, T)
        probs = odd.take(2, T)
        probsT = odd.take(2, T)
        spad = odd.take(CT, PADS + T)
        sxs = qsq[:, 0:2, :].rearrange("p a (c t) -> p (a c) t", c=2)
        sacc = qsq[:, 2:4, :].rearrange("p a (c t) -> p (a c) t", c=2)
        moe = Phase()
        hrT = moe.take(DT, T)
        grow = moe.take(D)
        disp = moe.take(TT, P)
        act = hrT[:, 0:4, :].rearrange("p (a b) t -> p a (b t)", a=2)
        ehid = hrT[:, 4:8, :].rearrange("p (a b) t -> p a (b t)", a=2)
        lg = moe.take(TT, 12, NE)

        ss = sb("ss", [P, 4, TT])
        rstd = sb("rstd", [P, 4, TT])
        vrow = cacc[:, 0, 0:P]
        drow = cacc[:, 1, 0:P]
        vcol = sb("vcol", [P, P])
        dcol = sb("dcol", [P, P])
        dround = sb("dround", [P, TAPS * CT], F32R)
        drest = sb("drest", [P, TAPS * CT])
        ident = sb("ident", [P, P])
        ones = sb("ones", [P, T])
        headmean = sb("headmean", [P, P // HD])
        lnmean = sb("lnmean", [P, P])
        before = sb("before", [P, P])
        identw = sb("identw", [P, 3 * P], F32R)
        causal = sb("causal", [P, 3 * P], F32R)
        pick = sb("pick", [FR, NH], F32R)
        eps = sb("eps", [P, 1])
        iota = sb("iota", [P, T])
        qkg = sb("qkg", [P, 2])
        fb = sb("fb", [FR, 1])
        wf = sb("wf", [P, DT, NH])
        rms_qk = sb("rms_qk", [P, TT, 2 * NH])
        rq = sb("rq", [P, TT, HR])
        wr = sb("wr", [P, DT, NE])
        rb = sb("rb", [P, NE])
        unused = sb("unused", [P, 16])
        rmax = sb("rmax", [P, 2 * NH, 4])
        idx = sb("idx", [P, TT, 8], mybir.dt.uint32)
        pos = sb("pos", [P, TT, 2 * NE + 1])
        comb = sb("comb", [P, TT, 2 * NE + 1])
        gslot = sb("gslot", [P, 1])
        cnt = sb("cnt", [P, 2])
        over = sb("over", [P, 1], I32)

        bank = [ctx.enter_context(nc.psum_tensor(f"bank{i}", [P, 512], F32)) for i in range(8)]

        loaded = [sem(f"loaded{s}") for s in range(RING)]
        hi_ready = sem("hi_ready")
        lo_ready = sem("lo_ready")
        sum_done = sem("sum_done")
        half_done = sem("half_done")
        vectors_loaded = sem("vectors_loaded")
        small_loaded = sem("small_loaded")
        grow_loaded = sem("grow_loaded")
        x_loaded = sem("x_loaded")
        pool_const = sem("pool_const")
        consts = sem("consts")
        dve_const = sem("dve_const")
        vec_turned = sem("vec_turned")
        vec_ready = sem("vec_ready")
        sq_done = sem("sq_done")
        rms_ready = sem("rms_ready")
        rstd_ready = sem("rstd_ready")
        normed_ready = sem("normed_ready")
        turned = sem("turned")
        xhi_ready = sem("xhi_ready")
        xlo_ready = sem("xlo_ready")
        sig_ready = sem("sig_ready")
        u_ready = sem("u_ready")
        xpad_ready = sem("xpad_ready")
        pool_step = sem("pool_step")
        pooled_ready = sem("pooled_ready")
        poolmix_done = sem("poolmix_done")
        conv_step = [sem(f"conv_step{j}") for j in range(CT)]
        tap_product = sem("tap_product")
        dround_ready = sem("dround_ready")
        drest_ready = sem("drest_ready")
        diag_ready = sem("diag_ready")
        tap_done = sem("tap_done")
        uhi_ready = sem("uhi_ready")
        ulo_ready = sem("ulo_ready")
        conv_ready = sem("conv_ready")
        mean_done = sem("mean_done")
        xc_ready = sem("xc_ready")
        csq_ready = sem("csq_ready")
        cvar_done = sem("cvar_done")
        crms_ready = sem("crms_ready")
        crstd_ready = sem("crstd_ready")
        cn_ready = sem("cn_ready")
        cout_ready = sem("cout_ready")
        resid_ready = sem("resid_ready")
        silu_ready = sem("silu_ready")
        hid_ready = sem("hid_ready")
        hhi_ready = sem("hhi_ready")
        hlo_ready = sem("hlo_ready")
        f_done = sem("f_done")
        f_step = sem("f_step")
        f_act = sem("f_act")
        f_ready = sem("f_ready")
        qsq_ready = sem("qsq_ready")
        qms_done = sem("qms_done")
        qrms_ready = sem("qrms_ready")
        qrstd_ready = sem("qrstd_ready")
        rq_zero = sem("rq_zero")
        rq_turned = sem("rq_turned")
        rqhi_ready = sem("rqhi_ready")
        rqlo_ready = sem("rqlo_ready")
        wide_ready = sem("wide_ready")
        spread = sem("spread")
        qr_copied = sem("qr_copied")
        wf_hi = sem("wf_hi")
        wf_lo = sem("wf_lo")
        qk_ready = sem("qk_ready")
        v_ready = sem("v_ready")
        sx_copied = sem("sx_copied")
        s_step = sem("s_step")
        z_ready = sem("z_ready")
        short_ready = sem("short_ready")
        short_hi = sem("short_hi")
        short_lo = sem("short_lo")
        score_done = sem("score_done")
        max_step = sem("max_step")
        max_ready = sem("max_ready")
        exp_ready = sem("exp_ready")
        p_step = sem("p_step")
        p_ready = sem("p_ready")
        pT_done = sem("pT_done")
        pT_ready = sem("pT_ready")
        o_done = sem("o_done")
        o_hi = sem("o_hi")
        o_lo = sem("o_lo")
        hr_lo = sem("hr_lo")
        hr_hi = sem("hr_hi")
        logits_done = sem("logits_done")
        r_step = sem("r_step")
        r_exp = sem("r_exp")
        mask_ready = sem("mask_ready")
        count_done = sem("count_done")
        over_ready = sem("over_ready")
        disp_ready = sem("disp_ready")
        gathered = sem("gathered")
        ehi_ready = sem("ehi_ready")
        elo_ready = sem("elo_ready")
        dispT_done = sem("dispT_done")
        dispT_ready = sem("dispT_ready")
        act_ready = sem("act_ready")
        ehid_ready = sem("ehid_ready")
        ehidT_done = sem("ehidT_done")
        ehidT_hi = sem("ehidT_hi")
        ehidT_lo = sem("ehidT_lo")
        yhi_ready = sem("yhi_ready")
        ylo_ready = sem("ylo_ready")
        scattered = sem("scattered")
        added = sem("added")
        out_ready = sem("out_ready")
        out_stored = sem("out_stored")

        rows, n = {}, 0
        for name, k in (("ev_norm_mix", DT), ("ev_norm_ffn", DT), ("od_norm_mix", DT), ("od_norm_ffn", DT),
                        ("pool_scale", CT), ("conv_dw_b", CT), ("conv_ln_g", CT), ("conv_ln_b", CT)):
            rows[name] = (n, k)
            n += k
        SCW = n
        NV = n + STAPS * CT
        ND = TAPS * CT

        def col(name, k):
            i = rows[name][0] + k
            return vcol[:, i:i + 1]

        norms = ("ev_norm_mix", "ev_norm_ffn", "od_norm_mix")
        VECTORS, SMALL = 16 * (len(rows) + 2), 16 * (8 + FR // NH)

        def view(u, k):
            return ring[:, u % RING, :].rearrange("p (k n) -> p k n", k=k)

        def half_shape(u):
            k = (units[u] if u < MOE else (None, (4 if expert_units[(u - MOE) % PER][2] is not None else 2)))[1]
            return (DT, P) if k == DT else (k // 2, UNIT // k)

        def raw_half(u, h):
            k, n_ = half_shape(u)
            if k == DT:
                return view(u, DT)[:, :, h * P:(h + 1) * P]
            return ring[:, u % RING, h * HALF:(h + 1) * HALF].rearrange("p (k n) -> p k n", k=k)

        def split_half(part, u, h):
            return part[:, (2 * u + h) % SPLITS, :].rearrange("p (k n) -> p k n", k=half_shape(u)[0])

        IDENTITIES = 5
        KEEP = (20, 24, 24, 36, 16)
        SHORT_BANKS = (7, 0, 1, 7)
        GTAPS = 14
        EARLY = 8

        def conv_tap(eng, s_, j):
            w = dcol[:, s_ * CT + j:s_ * CT + j + 1]
            src = upad[:, j, s_:s_ + T]
            if s_ == 0:
                ins = eng.tensor_scalar(cacc[:, j, :], src, w, col("conv_dw_b", j), ALU.mult, ALU.add)
            else:
                eng.wait_ge(conv_step[j], s_)
                ins = eng.scalar_tensor_tensor(out=cacc[:, j, :], in0=src, scalar=w, in1=cacc[:, j, :],
                                               op0=ALU.mult, op1=ALU.add)
            ins.then_inc(conv_step[j], 1)

        LOADS_PER = 16 * (PER // RING)
        ROUTER_STEPS = 2 + 2 * TT + 1

        def split_hi(eng, x, i=None):
            u, h = x // 2, x % 2
            if h == 0:
                eng.wait_ge(loaded[u % RING], 16 * (u // RING + 1) + (0 if i is None else i * LOADS_PER))
            if x >= SPLITS:
                eng.wait_ge(half_done, x - SPLITS + 1 + (0 if i is None else i * 2 * PER))
            eng.activation(split_half(whi, u, h), raw_half(u, h), ACT.Copy).then_inc(hi_ready, 1)

        def split_lo(eng, x, i=None):
            u, h = x // 2, x % 2
            eng.wait_ge(hi_ready, x + 1 + (0 if i is None else i * 2 * PER))
            eng.tensor_tensor(split_half(wlo, u, h), raw_half(u, h), split_half(whi, u, h).bitcast(F32),
                              ALU.subtract).then_inc(lo_ready, 1)

        def run(eng, expert):
            with eng.Fori(0, NE - 1) as i:
                expert(i, False)
            eng.wait_ge(over_ready, 1)
            more = eng.value_load(over[0:1, 0:1], min_val=0, max_val=1)
            with eng.If(more == 1):
                with eng.Fori(NE - 1, 2 * NE - 1) as i:
                    expert(i, False)
                expert(2 * NE - 1, True)
            with eng.Else():
                expert(NE - 1, True)

        block = ctx.enter_context(nc.Block())

        @block.sync
        def _(sp):
            sp.dma_start(resid[:, :, :], a["x"][0].rearrange("(t p) d -> p t d", p=P)).then_inc(x_loaded, 16)
            for name, (r, k) in rows.items():
                sp.dma_start(vrow[r:r + k, :], a[name][0].rearrange("(k p) -> k p", p=P)).then_inc(vectors_loaded, 16)
            sp.dma_start(vrow[SCW:NV, :], a["sc_conv_w"][0].rearrange("s (k p) -> (s k) p", p=P)).then_inc(vectors_loaded, 16)
            sp.dma_start(drow[0:ND, :], a["conv_dw_w"][0].rearrange("s (k p) -> (s k) p", p=P)).then_inc(vectors_loaded, 16)

            for u, (src, k, n_) in enumerate(units):
                if u >= RING:
                    sp.wait_ge(lo_ready, 2 * (u - RING + 1))
                sp.dma_start(view(u, k), src).then_inc(loaded[u % RING], 16)
                if u == 1:
                    for r in range(P // HD):
                        sp.dma_start(qkg[r * HD:(r + 1) * HD, 0:1], a["q_norm_g"].rearrange("a d -> d a")).then_inc(small_loaded, 16)
                        sp.dma_start(qkg[r * HD:(r + 1) * HD, 1:2], a["k_norm_g"].rearrange("a d -> d a")).then_inc(small_loaded, 16)
                    sp.dma_start(poolw, a["pool_w"][0].rearrange("g c d -> c g d")).then_inc(small_loaded, 16)
                    for r in range(FR // NH):
                        sp.dma_start(fb[r * NH:(r + 1) * NH, :], a["forget_bias"].rearrange("a h -> h a")).then_inc(small_loaded, 16)
                    sp.dma_start(wf[:, :, :], od_in[:, 3 * C:3 * C + NH].rearrange("(k p) n -> p k n", p=P)).then_inc(small_loaded, 16)
                    sp.dma_start(wr[:, :, :], a["router_w"][0].rearrange("(k p) n -> p k n", p=P)).then_inc(small_loaded, 16)
                    sp.dma_start(rb[:, :], a["router_b"][0:1, :].to_broadcast([P, NE])).then_inc(small_loaded, 16)

            def load_expert(i, e, j):
                name, k0, c0 = expert_units[j]
                u = MOE + j
                if c0 is None:
                    src = a[name][0][e, k0 * P:(k0 + 2) * P, :].rearrange("(k p) n -> p k n", p=P)
                else:
                    src = a[name][0][e, k0 * P:(k0 + 4) * P, c0:c0 + 512].rearrange("(k p) n -> p k n", p=P)
                sp.wait_ge(lo_ready, i * (2 * PER) + 2 * (u - RING + 1))
                sp.dma_start(view(u, 2 if c0 is None else 4), src).then_inc(loaded[u % RING], 16)

            with sp.Fori(0, NE) as i:
                for j in range(PER):
                    load_expert(i, i, j)
            sp.wait_ge(over_ready, 1)
            more = sp.value_load(over[0:1, 0:1], min_val=0, max_val=1)
            with sp.If(more == 1):
                with sp.Fori(NE, 2 * NE) as i:
                    for j in range(PER):
                        load_expert(i, i - NE, j)
            sp.wait_ge(out_ready, 4)
            sp.dma_start(out[0].rearrange("(t p) d -> p t d", p=P), resid[:, :, :]).then_inc(out_stored, 16)
            sp.wait_ge(out_stored, 16)

        @block.gpsimd
        def _(pool):
            n = [0]

            def chain(ins):
                n[0] += 1
                ins.then_inc(pool_const, 1)
                pool.wait_ge(pool_const, n[0])

            chain(pool.memset(eps[:, :], EPS))
            chain(pool.memset(ident[:, :], 0.0))
            chain(pool.affine_select(out=ident[:, :], in_=ident[:, :], compare_op=ALU.not_equal, fill=1.0, base=0,
                                     pattern=[[-1, P]], channel_multiplier=1))
            chain(pool.memset(identw[:, :].bitcast(F32), 0.0))
            chain(pool.affine_select(out=identw[:, :], in_=identw[:, :].bitcast(F32), compare_op=ALU.not_equal,
                                     fill=1.0, base=P, pattern=[[-1, 3 * P]], channel_multiplier=1))
            assert n[0] == IDENTITIES
            chain(pool.iota(iota[:, :], pattern=[[1, T]], base=0, channel_multiplier=0,
                            allow_small_or_imprecise_dtypes=True))
            pool.memset(upad, 0.0).then_inc(consts, 1)
            pool.memset(ones[:, :], 1.0).then_inc(consts, 1)
            pool.memset(lnmean[:, :], 1.0 / C).then_inc(consts, 1)
            chain(pool.memset(before[:, :], 1.0))
            chain(pool.affine_select(out=before[:, :], in_=before[:, :], compare_op=ALU.is_gt, fill=0.0, base=0,
                                     pattern=[[1, P]], channel_multiplier=-1))
            chain(pool.memset(causal[:, :].bitcast(F32), 0.0))
            chain(pool.affine_select(out=causal[:, P:2 * P], in_=causal[:, P:2 * P].bitcast(F32), compare_op=ALU.is_ge,
                                     fill=NEG, base=0, pattern=[[-1, P]], channel_multiplier=1))
            chain(pool.memset(pick[:, :].bitcast(F32), 0.0))
            for r in (0, 64):
                chain(pool.affine_select(out=pick[:, :], in_=pick[:, :].bitcast(F32), compare_op=ALU.not_equal,
                                         fill=1.0, base=-r, pattern=[[-1, NH]], channel_multiplier=1))
            chain(pool.memset(headmean[:, :], 0.0))
            for r in range(P // HD):
                pool.memset(headmean[r * HD:(r + 1) * HD, r:r + 1], 1.0 / HD).then_inc(consts, 1)
                pool.wait_ge(consts, 4 + r)

            pool.wait_ge(turned, 4)
            pool.memset(xpad, 0.0).then_inc(consts, 1)

            pool.wait_ge(u_ready, 1)
            conv_tap(pool, 0, 0)
            for s_ in range(1, GTAPS):
                pool.wait_ge(conv_step[0], s_)
                pool.tensor_scalar(ctmp, upad[:, 0, s_:s_ + T], dcol[:, s_ * CT:s_ * CT + 1], None,
                                   ALU.mult).then_inc(tap_product, 1)
                pool.wait_ge(tap_product, s_)
                pool.tensor_tensor(cacc[:, 0, :], cacc[:, 0, :], ctmp, ALU.add).then_inc(conv_step[0], 1)

            m = [0]

            def step(ins):
                m[0] += 1
                ins.then_inc(pool_step, 1)
                pool.wait_ge(pool_step, m[0])

            L = PADP + T
            pool.wait_ge(u_ready, 2)
            pool.wait_ge(xpad_ready, 2)
            step(pool.tensor_tensor(winA[:, :, 1:L], xpad[:, :, 1:L], xpad[:, :, 0:L - 1], ALU.add))
            step(pool.tensor_tensor(winB[:, 1:, 3:L], winA[:, 1:, 3:L], winA[:, 1:, 1:L - 2], ALU.add))
            step(pool.tensor_tensor(winA[:, 2:, 7:L], winB[:, 2:, 7:L], winB[:, 2:, 3:L - 4], ALU.add))
            step(pool.tensor_tensor(winB[:, 3, 15:L], winA[:, 3, 15:L], winA[:, 3, 7:L - 8], ALU.add))
            pool.wait_ge(dve_const, 2 * CT)
            for g in range(CT):
                w = (winA if g % 2 == 0 else winB)[:, g, PADP:L]
                step(pool.tensor_tensor(w, w, rcount[:, g, :], ALU.mult))
                pool.tensor_tensor(w, w, xpad[:, g, PADP:L], ALU.subtract).then_inc(pooled_ready, 1)
                pool.wait_ge(pooled_ready, g + 1)

            pool.wait_ge(half_done, 2 * O_IN)
            pool.memset(wfhi.bitcast(F32), 0.0).then_inc(wide_ready, 1)
            pool.memset(wflo[:, :, :].bitcast(F32), 0.0).then_inc(wide_ready, 1)
            chain(pool.memset(heads.bitcast(F32), 0.0))
            for k, r in enumerate((0, 32)):
                pool.affine_select(out=heads, in_=heads.bitcast(F32), compare_op=ALU.not_equal, fill=1.0, base=-r,
                                   pattern=[[-1, 2 * NH], [0, HD]], channel_multiplier=1).then_inc(wide_ready, 1)
                pool.wait_ge(wide_ready, k + 3)

        @block.scalar
        def _(s):
            cursor = [0]

            def splits_to(n_):
                while cursor[0] < n_:
                    split_hi(s, cursor[0])
                    cursor[0] += 1

            def after_half(n_):
                splits_to(n_ + AHEAD)
                s.wait_ge(half_done, n_)

            def table(func):
                s.activation(unused[:, tables[0]:tables[0] + 1], eps[:, 0:1], func)
                tables[0] += 1

            tables = [0]

            def squares(k):
                table(ACT.Sqrt)
                for t in range(TT):
                    if k:
                        s.wait_ge(resid_ready, 4 * (k - 1) + 2 * t + 2)
                    s.activation(normed[:, t, :], resid[:, t, :], ACT.Square, accum_out=ss[:, k, t:t + 1]).then_inc(sq_done, 1)
                s.wait_ge(sq_done, TT * (k + 1))
                s.activation(ss[:, k, :], ss[:, k, :], ACT.Sqrt, bias=eps[:, 0:1], scale=1.0 / D).then_inc(rms_ready, 1)

            def gain(k):
                for d in range(DT):
                    if d % 2 == 0:
                        s.wait_ge(turned, 4 * k + d // 2 + 1)
                    s.activation(xhi[:, d, :], bank[d // 2][:, (d % 2) * T:(d % 2 + 1) * T], ACT.Copy,
                                 scale=col(norms[k], d)).then_inc(xhi_ready, 1)

            s.wait_ge(pool_const, 1)
            s.wait_ge(x_loaded, 16)
            squares(0)
            splits_to(2)
            s.wait_ge(vec_ready, 2)
            gain(0)
            splits_to(SPLITS)
            s.activation(dround[:, :], dcol[:, 0:ND], ACT.Copy).then_inc(dround_ready, 1)

            def diagonals(n0, n1):
                for n_ in range(n0, n1):
                    i = (VTAPS + n_ % PTAPS) * CT + n_ // PTAPS
                    if n_ >= DIAGS:
                        s.wait_ge(tap_done, n_ - DIAGS + 1)
                    s.activation(diag_hi[:, n_ % DIAGS, :], ident[:, :], ACT.Copy, scale=dcol[:, i:i + 1]).then_inc(diag_ready, 1)
                    s.activation(diag_lo[:, n_ % DIAGS, :], ident[:, :], ACT.Copy, scale=drest[:, i:i + 1]).then_inc(diag_ready, 1)

            s.wait_ge(drest_ready, 1)
            for j in range(2):
                after_half(2 * (E_IN + 2 * j + 2))
                s.activation(sig[:, j, :], bank[5 + 2 * j][:, :], ACT.Sigmoid).then_inc(sig_ready, 1)
                diagonals(j * (DIAGS // 2), (j + 1) * (DIAGS // 2))
            s.wait_ge(consts, 6)
            for j in range(2):
                after_half(2 * (E_IN + 5 + j))
                if j == 1:
                    s.wait_ge(u_ready, 2)
                    for c in range(CT):
                        s.activation(u_part(0, c), upad[:, c, VTAPS:], ACT.Copy).then_inc(uhi_ready, 1)
                s.activation(xpad[:, 2 * j:2 * j + 2, PADP:], bank[j][:, :].rearrange("p (c t) -> p c t", c=2),
                             ACT.Copy).then_inc(xpad_ready, 1)
            splits_to(2 * E_OUT + SPLITS)
            diagonals(DIAGS, CT * PTAPS)
            table(ACT.Sqrt)
            for j in range(CT):
                s.wait_ge(pooled_ready, j + 1)
                s.wait_ge(xc_ready, j + 1)
                s.activation(csq[:, j, :], cacc[:, j, :], ACT.Square).then_inc(csq_ready, 1)
            for g in range(CT):
                s.wait_ge(poolmix_done, g // 2 + 1)
                s.activation(xhi[:, g, :], bank[2 + g // 2][:, (g % 2) * T:(g % 2 + 1) * T], ACT.Copy,
                             scale=col("pool_scale", g)).then_inc(xhi_ready, 1)
            s.wait_ge(cvar_done, 1)
            s.activation(crms[:, 0, :], bank[5][:, 0:T], ACT.Sqrt, bias=eps[:, 0:1]).then_inc(crms_ready, 1)
            table(ACT.Silu)
            for j in range(CT):
                s.wait_ge(cn_ready, j + 1)
                s.activation(csq[:, j, :], cacc[:, j, :], ACT.Silu, bias=col("conv_ln_b", j),
                             scale=col("conv_ln_g", j)).then_inc(cout_ready, 1)
                s.wait_ge(cout_ready, j + 1)
                s.activation(xhi[:, CT + j, :], csq[:, j, :], ACT.Copy).then_inc(xhi_ready, 1)
            splits_to(2 * FFN + 2)
            squares(1)
            gain(1)
            for j in range(FB):
                after_half(2 * (ffn_gate[j] + 1))
                if j >= 2:
                    s.wait_ge(hid_ready, j - 1)
                s.activation(gated[:, j % 2, :], bank[4 + j % 2][:, :], ACT.Silu).then_inc(silu_ready, 1)
                splits_to(2 * (ffn_up[j] + 1) + AHEAD)
                s.wait_ge(hid_ready, j + 1)
                if j >= 2:
                    s.wait_ge(half_done, 2 * (ffn_down[j - 2] + 1))
                s.activation(hhi[:, j % 2, :], hidden[:, j % 2, :], ACT.Copy).then_inc(hhi_ready, 1)
            splits_to(2 * O_IN + 2)
            squares(2)
            gain(2)
            s.wait_ge(small_loaded, SMALL)
            s.wait_ge(wide_ready, 1)
            for r in (0, 64):
                s.activation(wfhi[:, :, r:r + NH], wf[:, :, :], ACT.Copy).then_inc(wf_hi, 1)
            splits_to(2 * O_IN + SPLITS)
            s.wait_ge(f_step, 2)
            s.activation(fl[0:FR, 2, :], fl[0:FR, 1, :], ACT.Exp, scale=-1.0).then_inc(f_act, 1)
            s.wait_ge(f_act, 1)
            s.activation(fl[0:FR, 3, :], fl[0:FR, 2, :], ACT.Ln, bias=1.0).then_inc(f_act, 1)
            table(ACT.Sqrt)
            for m in range(4):
                after_half(2 * (O_Q + m + 1))
                s.activation(qsq[:, m, :], bank[4 + m][:, :], ACT.Square).then_inc(qsq_ready, 1)
            splits_to(2 * (O_V + 1) + AHEAD)
            s.wait_ge(qms_done, 1)
            s.activation(rms_qk[:, :, :], bank[2][:, 0:TT * 2 * NH].rearrange("p (t n) -> p t n", t=TT), ACT.Sqrt,
                         bias=eps[:, 0:1]).then_inc(qrms_ready, 1)
            s.wait_ge(rq_turned, 1)
            s.activation(rqT, bank[3][0:HR, 0:T], ACT.Copy).then_inc(rqhi_ready, 1)
            after_half(2 * (O_V + 2))
            for t in range(TT):
                s.activation(v[:, t, :], bank[t][:, :], ACT.Copy).then_inc(v_ready, 1)
            for j in range(2):
                after_half(2 * (O_SX + j + 1))
                s.wait_ge(qk_ready, j + 1)
                s.activation(sxs[:, 2 * j:2 * j + 2, :], bank[j][:, :].rearrange("p (c t) -> p c t", c=2),
                             ACT.Copy).then_inc(sx_copied, 1)

            def attention_hi(i):
                h, q = i // 2, i % 2
                r = (h % 2) * HD
                s.wait_ge(o_done, i + 1)
                s.activation(ohi[r:r + HD, h // 2, q * P:(q + 1) * P], bank[2 + i % 2][r:r + HD, 0:P],
                             ACT.Copy).then_inc(o_hi, 1)

            def short_part(j):
                s.wait_ge(short_ready, j + 1)
                s.activation(xhi[:, CT + j, :], sacc[:, j, :], ACT.Copy).then_inc(short_hi, 1)

            table(ACT.Exp)
            for i in range(2 * NH + 2):
                if i < 2 * NH:
                    nk = (i % 2 + 1) * P
                    s.wait_ge(max_ready, i + 1)
                    s.activation(probs[:, i % 2, 0:nk], bank[4 + i % 2][:, 0:nk], ACT.Exp, bias=rmax[:, i, 1:2],
                                 accum_out=rmax[:, i, 2:3]).then_inc(exp_ready, 1)
                if i >= 2:
                    attention_hi(i - 2)
                splits_to(2 * O_SC + i // 2 + AHEAD)
            s.dma_start(grow, a["od_norm_ffn"][0:1, :].to_broadcast([P, D])).then_inc(grow_loaded, 16)
            splits_to(2 * O_OUT + SPLITS)
            s.wait_ge(half_done, 2 * O_OUT)
            for j in range(CT):
                short_part(j)
            splits_to(2 * MOE + 2)
            squares(3)
            for n_ in range(DT // 2, DT):
                s.wait_ge(turned, 12 + n_ // 2 + 1)
                s.activation(hrT[:, n_, :], bank[n_ // 2][:, (n_ % 2) * T:(n_ % 2 + 1) * T], ACT.Copy,
                             scale=col("od_norm_ffn", n_)).then_inc(hr_hi, 1)
            table(ACT.Exp)
            s.wait_ge(r_step, ROUTER_STEPS)
            s.activation(lg[:, :, 10, 1], lg[:, :, 10, 0], ACT.Exp).then_inc(r_exp, 1)
            splits_to(2 * MOE + AHEAD)

            def gathered_hi(k):
                for h in range(2):
                    s.wait_ge(gathered, 2 * k + h + 1)
                    s.activation(xhi[:, 4 * h:4 * h + 4, 0:P], bank[(7, 1)[h]][:, :].rearrange("p (c t) -> p c t", c=4),
                                 ACT.Copy).then_inc(ehi_ready, 1)

            gathered_hi(0)

            def expert(i, last):
                mine = [2 * MOE + AHEAD]

                def more(n_):
                    while mine[0] < min(2 * MOE + n_, 2 * (MOE + PER) + (0 if last else AHEAD)):
                        split_hi(s, mine[0], i)
                        mine[0] += 1

                def after(n_):
                    more(n_ + AHEAD)
                    s.wait_ge(half_done, i * (2 * PER) + 2 * MOE + n_)

                for c in range(EB + 1):
                    if c < EB:
                        after(2 * (moe_gate[c] + 2))
                        s.wait_ge(ehid_ready, 1 + i * EB + max(c - 1, 0))
                        s.activation(act[:, c % 2, :], bank[c % 2][:, :], ACT.Silu).then_inc(act_ready, 1)
                    if c >= 1:
                        if c == EB:
                            more(2 * (moe_down[c - 2] + 2) + AHEAD)
                        s.wait_ge(ehidT_done, 1 + i * EB + c)
                        s.activation(hhi[:, (c - 1) % 2, :], bank[6][:, :], ACT.Copy).then_inc(ehidT_hi, 1)
                if not last:
                    gathered_hi(i + 1)
                after(2 * PER)
                s.wait_ge(dispT_ready, 2 * i + 2)
                for h in range(2):
                    s.activation(yhi[:, h, :, :], bank[4 + h][:, :].rearrange("p (c n) -> p c n", c=4), ACT.Copy,
                                 scale=gslot[:, 0:1]).then_inc(yhi_ready, 1)

            run(s, expert)

        @block.tensor
        def _(pe):
            def product(dst, lhs, rhs, start, stop):
                pe.matmul(dst, lhs[0], rhs[0], start=start, stop=False)
                pe.matmul(dst, lhs[0], rhs[1], start=False, stop=False)
                return pe.matmul(dst, lhs[1], rhs[0], start=False, stop=stop)

            def halves(u, i=None):
                for h in range(2):
                    x = 2 * u + h
                    pe.wait_ge(lo_ready, x + 1 + (0 if i is None else i * 2 * PER))
                    yield h, split_half(whi, u, h), split_half(wlo, u, h)

            def cols_half(u, c, wh, wl, b, tiles_before=None):
                for k in range(DT):
                    if tiles_before is not None:
                        pe.wait_ge(xlo_ready, tiles_before + k + 1)
                    mm = product(bank[b][:, c * T:(c + 1) * T], (wh[:, k, :], wl[:, k, :]),
                                 (xhi[:, k, :], xlo[:, k, :]), k == 0, k == DT - 1)
                mm.then_inc(half_done, 1)

            def cols_product(u, b, tiles_before=None):
                for c, wh, wl in halves(u):
                    cols_half(u, c, wh, wl, b, tiles_before if c == 0 else None)

            def rows_product(u, lhs, first, last):
                for k, wh, wl in halves(u):
                    for t in range(TT):
                        for h in range(2):
                            cols = slice(h * 512, (h + 1) * 512)
                            mm = product(bank[2 * t + h][:, :], lhs(k, t), (wh[:, 0, cols], wl[:, 0, cols]),
                                         first and k == 0, last and k == 1)
                            if last and k == 1 and (t, h) != (TT - 1, 1):
                                mm.then_inc(sum_done, 1)
                    mm.then_inc(half_done, 1)

            def keep_clock(n_, b=4):
                for _ in range(n_):
                    pe.matmul(bank[b][:, 0:T], identw[:, P:2 * P], identw[:, P:P + T], start=True, stop=True)

            def turn(k):
                keep_clock(KEEP[k])
                for b in range(4):
                    for c in range(2):
                        for t in range(TT):
                            d = 2 * b + c
                            if d == 0:
                                pe.wait_ge(normed_ready, TT * k + t + 1)
                            mm = pe.transpose(bank[b][:, c * T + t * P:c * T + (t + 1) * P],
                                              normed[:, t, d * P:(d + 1) * P], ident[:, :])
                    mm.then_inc(turned, 1)

            def out_product(u0, ms, tiles_before=None, source=(xhi, xlo)):
                for m in ms:
                    if tiles_before is not None:
                        pe.wait_ge(xlo_ready, tiles_before + 2 * m + 2)
                    rows_product(u0 + m, lambda k, t: tuple(x[:, 2 * m + k, t * P:(t + 1) * P] for x in source),
                                 m == 0, m == DT // 2 - 1)

            pe.wait_ge(pool_const, 3)
            pe.wait_ge(vectors_loaded, VECTORS)
            pe.transpose(bank[7][:, 0:NV], vrow[0:NV, :], ident[0:NV, 0:NV]).then_inc(vec_turned, 1)
            pe.transpose(bank[6][:, 0:ND], drow[0:ND, :], ident[0:ND, 0:ND]).then_inc(vec_turned, 1)
            pe.wait_ge(pool_const, IDENTITIES)
            turn(0)
            pe.wait_ge(vec_ready, 2)
            for m, b in enumerate((4, 5, 6, 7, 0, 1)):
                cols_product(E_IN + m, b, 0 if m == 0 else None)
            for j in range(CT):
                pe.wait_ge(ulo_ready, j + 1)
                for t in range(PTAPS):
                    n_ = j * PTAPS + t
                    pe.wait_ge(diag_ready, 2 * n_ + 2)
                    product(bank[6 + j // 2][:, (j % 2) * T:(j % 2 + 1) * T],
                            (diag_hi[:, n_ % DIAGS, :], diag_lo[:, n_ % DIAGS, :]),
                            (u_part(0, j)[:, t:t + T], u_part(1, j)[:, t:t + T]),
                            t == 0, t == PTAPS - 1).then_inc(tap_done, 1)
            for j in range(CT):
                pe.wait_ge(conv_ready, j // 2 + 1)
                mm = pe.matmul(bank[4][:, 0:T], lnmean[:, :], cacc[:, j, :], start=(j == 0), stop=(j == CT - 1))
            mm.then_inc(mean_done, 1)
            pe.wait_ge(small_loaded, SMALL)
            for g in range(CT):
                pe.wait_ge(pooled_ready, g + 1)
                w = (winA if g % 2 == 0 else winB)[:, g, PADP:]
                mm = pe.matmul(bank[2 + g // 2][:, (g % 2) * T:(g % 2 + 1) * T], poolw[:, g, :], w, start=True, stop=True)
                if g % 2:
                    mm.then_inc(poolmix_done, 1)
            for j in range(CT):
                pe.wait_ge(csq_ready, j + 1)
                mm = pe.matmul(bank[5][:, 0:T], lnmean[:, :], csq[:, j, :], start=(j == 0), stop=(j == CT - 1))
            mm.then_inc(cvar_done, 1)
            pe.wait_ge(xlo_ready, DT + CT)
            out_product(E_OUT, range(CT // 2))
            out_product(E_OUT, range(CT // 2, DT // 2), DT)

            pe.wait_ge(resid_ready, 4)
            turn(1)
            for j in range(FB + 1):
                if j < FB:
                    if j >= 2:
                        pe.wait_ge(hid_ready, j - 1)
                    cols_product(ffn_gate[j], 4 + j % 2, 2 * DT if j == 0 else None)
                    cols_product(ffn_up[j], 6 + j % 2)
                if j >= 1:
                    pe.wait_ge(hlo_ready, j)
                    rows_product(ffn_down[j - 1],
                                 lambda k, t: tuple(x[:, (j - 1) % 2, k * T + t * P:k * T + (t + 1) * P] for x in (hhi, hlo)),
                                 j == 1, j == FB)

            pe.wait_ge(resid_ready, 8)
            turn(2)
            cols_product(O_Q, 4, 3 * DT)
            pe.wait_ge(wf_lo, 2)
            for k in range(DT):
                mm = product(bank[2][0:FR, 0:T], (wfhi[:, k, :], wflo[:, k, :]), (xhi[:, k, :], xlo[:, k, :]), k == 0, k == DT - 1)
            mm.then_inc(f_done, 1)
            for m in range(1, 4):
                cols_product(O_Q + m, 4 + m)

            def v_half(u, h, wh, wl):
                for k in range(2):
                    for t in range(TT):
                        kk = 4 * u + 2 * h + k
                        mm = product(bank[t][:, :], tuple(x[:, kk, t * P:(t + 1) * P] for x in (xhi, xlo)),
                                     (wh[:, k, :], wl[:, k, :]), kk == 0, kk == DT - 1)
                mm.then_inc(half_done, 1)

            for h, wh, wl in halves(O_V):
                v_half(0, h, wh, wl)
            pe.wait_ge(f_step, 1)
            for m in range(4):
                pe.wait_ge(qsq_ready, m + 1)
                for c in range(2):
                    for t in range(TT):
                        n_ = t * 2 * NH + (2 * m + c) * (P // HD)
                        mm = pe.matmul(bank[2][:, n_:n_ + P // HD],
                                       qsq[:, m, c * T + t * P:c * T + (t + 1) * P], headmean[:, :], start=True, stop=True)
            mm.then_inc(qms_done, 1)
            for h, wh, wl in halves(O_V + 1):
                v_half(1, h, wh, wl)
                if h == 0:
                    pe.wait_ge(qrstd_ready, 2)
                    for t in range(TT):
                        mm = pe.transpose(bank[3][0:HR, t * P:(t + 1) * P], rq[:, t, :], ident[:, :])
                    mm.then_inc(rq_turned, 1)

            def spread_rq(m):
                if m >= 2:
                    pe.wait_ge(qk_ready, m - 1)
                for c in range(2):
                    mm = pe.matmul(bank[2 + m % 2][:, c * T:(c + 1) * T], heads[:, (2 * m + c) * P:(2 * m + c + 1) * P], rqT,
                                   start=True, stop=True)
                mm.then_inc(spread, 1)

            pe.wait_ge(rqlo_ready, 1)
            pe.wait_ge(wide_ready, 4)
            spread_rq(0)
            spread_rq(1)
            pe.wait_ge(v_ready, TT)
            cols_product(O_SX, 0)
            spread_rq(2)
            spread_rq(3)
            cols_product(O_SX + 1, 1)

            pe.wait_ge(f_ready, 4)
            pe.wait_ge(qk_ready, 4)

            def scores(i):
                h, q = i // 2, i % 2
                nk, r = (q + 1) * P, (h % 2) * HD
                b = bank[4 + i % 2]
                if i >= 2:
                    pe.wait_ge(exp_ready, i - 1)
                qh = qkT[r:r + HD, h // 4, (h // 2) % 2, q * P:(q + 1) * P]
                kh = qkT[r:r + HD, 2 + h // 4, (h // 2) % 2, 0:nk]
                w = pick[:, h:h + 1]
                pe.matmul(b[:, 0:T], identw[:, P:2 * P], causal[:, P - q * P:P - q * P + T], start=True, stop=False)
                pe.matmul(b[:, 0:nk], qh, kh, start=False, stop=False)
                pe.matmul(b[:, 0:T], fsum[:, q * P:(q + 1) * P], w.to_broadcast([FR, T]), start=False, stop=False)
                pe.matmul(b[:, 0:T], w.to_broadcast([FR, P]), fneg[:, 0:T], start=False, stop=True).then_inc(score_done, 1)

            def turn_probs(i):
                nk = (i % 2 + 1) * P
                pe.wait_ge(p_ready, i + 1)
                if i >= 1:
                    pe.wait_ge(pT_ready, i)
                for c in range(nk // P):
                    mm = pe.transpose(bank[6][:, c * P:(c + 1) * P], probs[:, i % 2, c * P:(c + 1) * P], ident[:, :])
                mm.then_inc(pT_done, 1)

            def attend(i):
                h, q = i // 2, i % 2
                r = (h % 2) * HD
                pe.wait_ge(pT_ready, i + 1)
                if i >= 2:
                    pe.wait_ge(o_lo, i - 1)
                for c in range(q + 1):
                    mm = pe.matmul(bank[2 + i % 2][r:r + HD, 0:P], v[:, c, h * HD:(h + 1) * HD],
                                   probsT[:, i % 2, c * P:(c + 1) * P], start=(c == 0), stop=(c == q))
                mm.then_inc(o_done, 1)

            for i in range(2 * NH + 2):
                if i < 2 * NH:
                    scores(i)
                if i % 2 == 0 and i < 2 * NH:
                    n_, h = i // 4, (i // 2) % 2
                    if h == 0 and n_ in (1, 2):
                        pe.wait_ge(sx_copied, n_)
                    if h == 0 and n_ == 3:
                        pe.wait_ge(z_ready, 2)
                    x = 2 * (O_SC + n_) + h
                    pe.wait_ge(lo_ready, x + 1)
                    cols_half(O_SC + n_, h, split_half(whi, O_SC + n_, h), split_half(wlo, O_SC + n_, h), SHORT_BANKS[n_])
                if 1 <= i <= 2 * NH:
                    turn_probs(i - 1)
                if i >= 2:
                    attend(i - 2)
            pe.wait_ge(o_lo, 2 * NH)
            out_product(O_OUT, range(CT // 2), source=(ohi, olo))
            pe.wait_ge(short_lo, CT)
            out_product(O_OUT, range(CT // 2, DT // 2))

            turn(3)
            for t in range(TT):
                for k in range(DT):
                    if t == 0:
                        pe.wait_ge(hr_lo if k < DT // 2 else hr_hi, k % (DT // 2) + 1)
                    mm = pe.matmul(bank[4 + t][:, 0:NE], hrT[:, k, t * P:(t + 1) * P], wr[:, k, :],
                                   start=(k == 0), stop=(k == DT - 1))
                mm.then_inc(logits_done, 1)
            keep_clock(KEEP[4], 6)
            pe.wait_ge(mask_ready, 1)
            pe.matmul(bank[6][:, 0:NE], before[:, :], lg[:, 0, 8, :], start=True, stop=True).then_inc(count_done, 1)
            pe.matmul(bank[7][:, 0:NE], ones[:, 0:P], lg[:, 0, 8, :], start=True, stop=False)
            pe.matmul(bank[7][:, 0:NE], before[:, :], lg[:, 1, 8, :], start=False, stop=True).then_inc(count_done, 1)
            pe.matmul(bank[5][:, 0:NE], ones[:, 0:P], lg[:, 0, 8, :], start=True, stop=False)
            pe.matmul(bank[5][:, 0:NE], ones[:, 0:P], lg[:, 1, 8, :], start=False, stop=True).then_inc(count_done, 1)

            def gather(k):
                pe.wait_ge(disp_ready, 2 * k + 2)
                for h in range(2):
                    for c in range(4):
                        for t in range(TT):
                            d = 4 * h + c
                            mm = pe.matmul(bank[(7, 1)[h]][:, c * P:(c + 1) * P], normed[:, t, d * P:(d + 1) * P],
                                           disp[:, t, :], start=(t == 0), stop=(t == TT - 1))
                    mm.then_inc(gathered, 1)

            pe.wait_ge(normed_ready, TT * 5)
            gather(0)
            for free in (dispT_done, ehidT_done):
                pe.sem_inc(free, 1)

            def expert(i, last):
                def up_product(j, b):
                    for g in range(2):
                        for h, wh, wl in halves(MOE + j + g, i):
                            for k in range(2):
                                kk = 4 * g + 2 * h + k
                                mm = product(bank[b][:, :], (xhi[:, kk, 0:P], xlo[:, kk, 0:P]),
                                             (wh[:, k, :], wl[:, k, :]), kk == 0, kk == DT - 1)
                            mm.then_inc(half_done, 1)

                pe.wait_ge(elo_ready, i * 2 + 2)
                for c in range(EB + 1):
                    if c < EB:
                        pe.wait_ge(ehid_ready, 1 + i * EB + max(c - 1, 0))
                        if c == 1:
                            pe.wait_ge(added, 1 + i * 4)
                        up_product(moe_gate[c], c % 2)
                    if c == 1:
                        for t in range(TT):
                            pe.transpose(bank[7][:, t * P:(t + 1) * P], disp[:, t, :], ident[:, :])
                        for t in range(TT):
                            mm = pe.matmul(bank[7][:, T:T + 1], disp[:, t, :], comb[:, t, bass.ds(i, 1)],
                                           start=(t == 0), stop=(t == TT - 1))
                        mm.then_inc(dispT_done, 1)
                    if c >= 1:
                        pe.wait_ge(ehid_ready, 1 + i * EB + c)
                        pe.wait_ge(ehidT_lo, 1 + i * EB + c - 1)
                        for f in range(4):
                            mm = pe.transpose(bank[6][:, f * P:(f + 1) * P], ehid[:, (c - 1) % 2, f * P:(f + 1) * P],
                                              ident[:, :])
                        mm.then_inc(ehidT_done, 1)
                    if c == EB and not last:
                        pe.wait_ge(dispT_ready, 2 * i + 2)
                        gather(i + 1)
                    if c < EB:
                        up_product(moe_up[c], 2 + c % 2)
                    if c >= 1:
                        pe.wait_ge(ehidT_lo, 1 + i * EB + c)
                        if c == 1:
                            pe.wait_ge(ylo_ready, 1 + i * 2)
                        for g in range(2):
                            for h, wh, wl in halves(MOE + moe_down[c - 1] + g, i):
                                for n_ in range(2):
                                    cols = slice(n_ * 512, (n_ + 1) * 512)
                                    f = (2 * g + h) * P
                                    mm = product(bank[4 + n_][:, :],
                                                 tuple(x[:, (c - 1) % 2, f:f + P] for x in (hhi, hlo)),
                                                 (wh[:, 0, cols], wl[:, 0, cols]), c == 1 and g == 0 and h == 0,
                                                 c == EB and g == 1 and h == 1)
                                mm.then_inc(half_done, 1)
                if not last:
                    pe.wait_ge(elo_ready, i * 2 + 4)
                for h in range(2):
                    pe.wait_ge(ylo_ready, 1 + i * 2 + h + 1)
                    for t in range(TT):
                        b = bank[(1, 3, 6, 7)[2 * h + t]]
                        pe.matmul(b[:, :], dispT[:, t, :], yhi[:, h, :, :], start=True, stop=False)
                        pe.matmul(b[:, :], dispT[:, t, :], ylo[:, h, :, :], start=False,
                                  stop=True).then_inc(scattered, 1)

            run(pe, expert)

        @block.vector
        def _(d):
            cursor = [0]

            def splits_to(n_):
                while cursor[0] < n_:
                    split_lo(d, cursor[0])
                    cursor[0] += 1

            def after_half(n_):
                splits_to(n_ + AHEAD)
                d.wait_ge(half_done, n_)

            d.wait_ge(vec_turned, 2)
            d.tensor_copy(vcol[:, 0:NV], bank[7][:, 0:NV]).then_inc(vec_ready, 1)
            d.tensor_copy(dcol[:, 0:ND], bank[6][:, 0:ND]).then_inc(vec_ready, 1)

            def normalize(k):
                d.wait_ge(rms_ready, k + 1)
                d.reciprocal(rstd[:, k, :], ss[:, k, :]).then_inc(rstd_ready, 1)
                d.wait_ge(rstd_ready, k + 1)
                for t in range(TT):
                    d.tensor_scalar(normed[:, t, :], resid[:, t, :], rstd[:, k, t:t + 1], None, ALU.mult).then_inc(normed_ready, 1)

            def scaled_lo(dst, src, scale, hi):
                return d.scalar_tensor_tensor(out=dst, in0=src, scalar=scale, in1=hi.bitcast(F32), op0=ALU.mult,
                                              op1=ALU.subtract)

            def gain(k):
                for n_ in range(DT):
                    if n_ % 2 == 0:
                        d.wait_ge(xhi_ready, DT * (k if k == 0 else k + 1) + n_ + 2)
                    scaled_lo(xlo[:, n_, :], bank[n_ // 2][:, (n_ % 2) * T:(n_ % 2 + 1) * T], col(norms[k], n_),
                              xhi[:, n_, :]).then_inc(xlo_ready, 1)

            sums = [0]

            def residual(u):
                splits_to(2 * u + 2)
                for t in range(TT):
                    for h in range(2):
                        if (t, h) != (TT - 1, 1):
                            sums[0] += 1
                            d.wait_ge(sum_done, sums[0])
                        else:
                            d.wait_ge(half_done, 2 * u)
                        r = resid[:, t, h * 512:(h + 1) * 512]
                        d.tensor_tensor(r, r, bank[2 * t + h][:, :], ALU.add).then_inc(resid_ready, 1)

            d.wait_ge(x_loaded, 16)
            normalize(0)
            splits_to(2)
            d.wait_ge(vec_ready, 2)
            gain(0)
            splits_to(SPLITS)
            d.wait_ge(dround_ready, 1)
            d.tensor_tensor(drest[:, :], dcol[:, 0:ND], dround[:, :].bitcast(F32), ALU.subtract).then_inc(drest_ready, 1)

            for g, w in enumerate(WINDOWS):
                if g == 0:
                    d.wait_ge(pool_const, 6)
                d.tensor_scalar(rcount[:, g, :], iota[:, :], 1.0, float(w), ALU.add, ALU.min).then_inc(dve_const, 1)

            def rcount_inverse(g):
                d.wait_ge(dve_const, g + 1)
                d.reciprocal(rcount[:, g, :], rcount[:, g, :]).then_inc(dve_const, 1)

            d.wait_ge(consts, 1)
            for j in range(2):
                splits_to(2 * (E_IN + 2 * j + 2) + AHEAD)
                d.wait_ge(sig_ready, j + 1)
                d.tensor_tensor(upad[:, 2 * j:2 * j + 2, PADC:], bank[4 + 2 * j][:, :].rearrange("p (c t) -> p c t", c=2),
                                sig[:, j, :].rearrange("p (c t) -> p c t", c=2), ALU.mult).then_inc(u_ready, 1)
                d.wait_ge(u_ready, j + 1)
                if j == 0:
                    for g in range(CT):
                        rcount_inverse(g)
                        splits_to(cursor[0] + 1)
                        conv_tap(d, g, 1)
                else:
                    for s_ in range(EARLY):
                        conv_tap(d, s_ + CT, 1)
                        conv_tap(d, s_, 2)
                        conv_tap(d, s_, 3)
                        if s_ % 2 and cursor[0] < 2 * E_OUT:
                            splits_to(cursor[0] + 1)
            splits_to(2 * E_OUT)
            for j in range(CT):
                d.wait_ge(uhi_ready, j + 1)
                d.tensor_tensor(u_part(1, j), upad[:, j, VTAPS:], u_part(0, j).bitcast(F32), ALU.subtract).then_inc(ulo_ready, 1)
            for s_ in range(EARLY, VTAPS):
                if s_ + CT < VTAPS:
                    conv_tap(d, s_ + CT, 1)
                conv_tap(d, s_, 2)
                conv_tap(d, s_, 3)
                if s_ >= GTAPS:
                    conv_tap(d, s_, 0)

            def add_taps(g):
                d.wait_ge(tap_done, (2 * g + 2) * PTAPS)
                for j in (2 * g, 2 * g + 1):
                    d.wait_ge(conv_step[j], VTAPS)
                r = cacc[:, 2 * g:2 * g + 2, :]
                d.tensor_tensor(r, r, bank[6 + g][:, :].rearrange("p (c t) -> p c t", c=2), ALU.add).then_inc(conv_ready, 1)

            add_taps(0)
            add_taps(1)
            splits_to(2 * E_OUT + 3)
            d.wait_ge(mean_done, 1)
            for j in range(CT):
                d.wait_ge(conv_ready, j // 2 + 1)
                d.tensor_tensor(cacc[:, j, :], cacc[:, j, :], bank[4][:, 0:T], ALU.subtract).then_inc(xc_ready, 1)
            splits_to(2 * E_OUT + SPLITS)
            for g in range(CT):
                d.wait_ge(xhi_ready, DT + (g // 2) * 2 + 2)
                scaled_lo(xlo[:, g, :], bank[2 + g // 2][:, (g % 2) * T:(g % 2 + 1) * T], col("pool_scale", g),
                          xhi[:, g, :]).then_inc(xlo_ready, 1)
            d.wait_ge(crms_ready, 1)
            d.reciprocal(crms[:, 1, :], crms[:, 0, :]).then_inc(crstd_ready, 1)
            d.wait_ge(crstd_ready, 1)
            for j in range(CT):
                d.wait_ge(xc_ready, j + 1)
                d.wait_ge(csq_ready, j + 1)
                d.tensor_tensor(cacc[:, j, :], cacc[:, j, :], crms[:, 1, :], ALU.mult).then_inc(cn_ready, 1)
            for j in range(CT):
                d.wait_ge(xhi_ready, DT + CT + j + 1)
                d.tensor_tensor(xlo[:, CT + j, :], csq[:, j, :], xhi[:, CT + j, :].bitcast(F32), ALU.subtract).then_inc(xlo_ready, 1)

            residual(FFN)
            normalize(1)
            gain(1)
            for j in range(FB):
                splits_to(2 * (ffn_gate[j] + 1) + AHEAD)
                after_half(2 * (ffn_up[j] + 1))
                d.wait_ge(silu_ready, j + 1)
                if j >= 2:
                    d.wait_ge(hhi_ready, j - 1)
                d.tensor_tensor(hidden[:, j % 2, :], gated[:, j % 2, :], bank[6 + j % 2][:, :], ALU.mult).then_inc(hid_ready, 1)
                if j >= 2:
                    d.wait_ge(half_done, 2 * (ffn_down[j - 2] + 1))
                d.wait_ge(hhi_ready, j + 1)
                d.tensor_tensor(hlo[:, j % 2, :], hidden[:, j % 2, :], hhi[:, j % 2, :].bitcast(F32),
                                ALU.subtract).then_inc(hlo_ready, 1)
            residual(O_IN)
            normalize(2)
            gain(2)
            splits_to(2 * O_IN + SPLITS)
            d.memset(rq[:, :, :], 0.0).then_inc(rq_zero, 1)
            d.wait_ge(wide_ready, 2)
            for k, r in enumerate((0, 64)):
                d.wait_ge(wf_hi, k + 1)
                d.tensor_tensor(wflo[:, :, r:r + NH], wf[:, :, :], wfhi[:, :, r:r + NH].bitcast(F32),
                                ALU.subtract).then_inc(wf_lo, 1)
            z, az, lse, F_ = (fl[0:FR, k, :] for k in (0, 1, 3, 1))
            d.wait_ge(f_done, 1)
            d.wait_ge(small_loaded, SMALL)
            d.tensor_scalar(z, bank[2][0:FR, 0:T], fb[:, 0:1], None, ALU.add).then_inc(f_step, 1)
            d.wait_ge(f_step, 1)
            d.scalar_tensor_tensor(out=az, in0=z, scalar=-1.0, in1=z, op0=ALU.mult, op1=ALU.max).then_inc(f_step, 1)
            d.wait_ge(f_act, 2)
            d.scalar_tensor_tensor(out=z, in0=z, scalar=0.0, in1=lse, op0=ALU.min, op1=ALU.subtract).then_inc(f_step, 1)
            d.wait_ge(f_step, 3)
            d.tensor_tensor_scan(F_, ones[0:FR, :], z, 0.0, ALU.mult, ALU.add).then_inc(f_ready, 1)
            d.wait_ge(f_ready, 1)
            d.tensor_copy(fsum, F_).then_inc(f_ready, 1)
            d.wait_ge(f_ready, 2)
            d.tensor_tensor(fsum[64:FR, :], F_[64:FR, :], fsum[64:FR, :].bitcast(F32), ALU.subtract).then_inc(f_ready, 1)
            d.wait_ge(f_ready, 3)
            d.tensor_scalar(fneg, fsum.bitcast(F32), -1.0, None, ALU.mult).then_inc(f_ready, 1)
            d.tensor_scalar(qkg[:, 0:1], qkg[:, 0:1], float(HD) ** -0.5, None, ALU.mult).then_inc(f_ready, 1)
            splits_to(2 * (O_V + 1) + AHEAD)
            d.wait_ge(qrms_ready, 1)
            d.wait_ge(rq_zero, 1)
            for r in (0, 32):
                d.reciprocal(rq[:, :, r:r + 2 * NH], rms_qk[:, :, :]).then_inc(qrstd_ready, 1)
            d.wait_ge(rqhi_ready, 1)
            d.tensor_tensor(rqT[32:HR, :], bank[3][32:HR, 0:T], rqT[32:HR, :].bitcast(F32), ALU.subtract).then_inc(rqlo_ready, 1)
            splits_to(2 * (O_V + 2) + AHEAD)
            d.wait_ge(f_ready, 5)
            for m in range(4):
                if m == 2:
                    splits_to(2 * (O_SX + 1) + AHEAD)
                d.wait_ge(spread, m + 1)
                d.tensor_copy(qsq[:, m, :], bank[2 + m % 2][:, :]).then_inc(qr_copied, 1)
                d.wait_ge(qr_copied, m + 1)
                d.scalar_tensor_tensor(out=qkT[:, m, :, :].rearrange("p c t -> p (c t)"), in0=bank[4 + m][:, :],
                                       scalar=qkg[:, m // 2:m // 2 + 1], in1=qsq[:, m, :], op0=ALU.mult,
                                       op1=ALU.mult).then_inc(qk_ready, 1)
            splits_to(2 * (O_SX + 2) + AHEAD)
            d.memset(spad[:, :, 0:PADS], 0.0).then_inc(z_ready, 1)

            def short_in(j):
                d.wait_ge(half_done, 2 * (O_SC + j + 1))
                d.wait_ge(sx_copied, j + 1)
                d.tensor_tensor(spad[:, 2 * j:2 * j + 2, PADS:],
                                bank[SHORT_BANKS[j]][:, :].rearrange("p (c t) -> p c t", c=2),
                                sxs[:, 2 * j:2 * j + 2, :], ALU.mult).then_inc(z_ready, 1)

            short = [(s_, 2 * g + j) for g in range(2) for s_ in range(STAPS) for j in range(2)]

            def short_count(s_, j):
                return short.index((s_, j)) + 1

            def short_tap(s_, j):
                w = vcol[:, SCW + s_ * CT + j:SCW + s_ * CT + j + 1]
                src = spad[:, j, s_:s_ + T]
                if s_ == 0:
                    d.wait_ge(z_ready, j // 2 + 2)
                    ins = d.tensor_scalar(sacc[:, j, :], src, w, None, ALU.mult)
                else:
                    d.wait_ge(s_step, short_count(s_ - 1, j))
                    ins = d.scalar_tensor_tensor(out=sacc[:, j, :], in0=src, scalar=w, in1=sacc[:, j, :],
                                                 op0=ALU.mult, op1=ALU.add)
                ins.then_inc(s_step, 1)

            def short_gate(j):
                d.wait_ge(half_done, 2 * (O_SB + j // 2 + 1))
                d.wait_ge(s_step, short_count(STAPS - 1, j))
                d.tensor_tensor(sacc[:, j, :], sacc[:, j, :],
                                bank[SHORT_BANKS[2 + j // 2]][:, (j % 2) * T:(j % 2 + 1) * T],
                                ALU.mult).then_inc(short_ready, 1)

            def short_rest(j):
                d.wait_ge(short_hi, j + 1)
                d.tensor_tensor(xlo[:, CT + j, :], sacc[:, j, :], xhi[:, CT + j, :].bitcast(F32),
                                ALU.subtract).then_inc(short_lo, 1)

            def softmax_max(i):
                nk = (i % 2 + 1) * P
                d.wait_ge(score_done, i + 1)
                d.tensor_reduce(rmax[:, i, 0:1], bank[4 + i % 2][:, 0:nk], AX.X, ALU.max).then_inc(max_step, 1)
                d.wait_ge(max_step, i + 1)
                d.tensor_scalar(rmax[:, i, 1:2], rmax[:, i, 0:1], -1.0, None, ALU.mult).then_inc(max_ready, 1)

            def softmax_norm(i):
                nk = (i % 2 + 1) * P
                d.wait_ge(exp_ready, i + 1)
                d.reciprocal(rmax[:, i, 3:4], rmax[:, i, 2:3]).then_inc(p_step, 1)
                d.wait_ge(p_step, i + 1)
                d.tensor_scalar(probs[:, i % 2, 0:nk], probs[:, i % 2, 0:nk], rmax[:, i, 3:4], None,
                                ALU.mult).then_inc(p_ready, 1)

            def copy_pT(i):
                nk = (i % 2 + 1) * P
                d.wait_ge(pT_done, i + 1)
                d.tensor_copy(probsT[:, i % 2, 0:nk], bank[6][:, 0:nk]).then_inc(pT_ready, 1)

            def attention_lo(i):
                h, q = i // 2, i % 2
                r = (h % 2) * HD
                d.wait_ge(o_hi, i + 1)
                d.tensor_tensor(olo[r:r + HD, h // 2, q * P:(q + 1) * P], bank[2 + i % 2][r:r + HD, 0:P],
                                ohi[r:r + HD, h // 2, q * P:(q + 1) * P].bitcast(F32), ALU.subtract).then_inc(o_lo, 1)

            for i in range(2 * NH + 2):
                if i < 2 * NH:
                    softmax_max(i)
                if i in (3, 7):
                    short_in((i - 3) // 4)
                first = 2 * (i - 4) if i < 7 else 2 * (i - 5)
                if 4 <= i < 7 or 8 <= i < 11:
                    short_tap(*short[first])
                    short_tap(*short[first + 1])
                if i in (12, 2 * NH):
                    for j in range(2):
                        short_gate(j + (0 if i == 12 else 2))
                if i < 2 * NH:
                    softmax_norm(i)
                if 1 <= i <= 2 * NH:
                    copy_pT(i - 1)
                if i >= 2:
                    attention_lo(i - 2)
                splits_to(2 * O_SC + i // 2 + AHEAD)
            splits_to(2 * O_OUT + SPLITS)
            for j in range(CT):
                short_rest(j)
            residual(MOE)
            normalize(3)
            for n_ in range(DT // 2):
                d.wait_ge(turned, 12 + n_ // 2 + 1)
                d.tensor_scalar(hrT[:, n_, :], bank[n_ // 2][:, (n_ % 2) * T:(n_ % 2 + 1) * T], col("od_norm_ffn", n_),
                                None, ALU.mult).then_inc(hr_lo, 1)
            d.wait_ge(grow_loaded, 16)
            d.wait_ge(turned, 16)
            for t in range(TT):
                d.tensor_tensor(normed[:, t, :], normed[:, t, :], grow, ALU.mult).then_inc(normed_ready, 1)

            r = [0]

            def chain(ins):
                r[0] += 1
                ins.then_inc(r_step, 1)
                d.wait_ge(r_step, r[0])

            chain(d.memset(pos[:, :, 2 * NE:], -1.0))
            chain(d.memset(comb[:, :, 2 * NE:], 0.0))
            d.wait_ge(logits_done, TT)
            for t in range(TT):
                chain(d.tensor_tensor(lg[:, t, 0, :], bank[4 + t][:, 0:NE], rb[:, :], ALU.add))
            for t in range(TT):
                chain(d.max(lg[:, t, 1, :], lg[:, t, 0, :]))
            chain(d.tensor_tensor(lg[:, :, 10, 0], lg[:, :, 1, 1], lg[:, :, 1, 0], ALU.subtract))
            assert r[0] == ROUTER_STEPS
            for t in range(TT):
                chain(d.max_index(idx[:, t, :], lg[:, t, 1, :], lg[:, t, 0, :]))
            chain(d.tensor_copy(lg[:, :, 2, 0:2], idx[:, :, 0:2]))
            for t in range(TT):
                for k in range(2):
                    chain(d.tensor_scalar(lg[:, t, 3 + k, :], iota[:, 0:NE], lg[:, t, 2, k:k + 1], None, ALU.is_equal))
            d.tensor_tensor(lg[:, :, 8, :], lg[:, :, 3, :], lg[:, :, 4, :], ALU.add).then_inc(mask_ready, 1)
            d.wait_ge(r_exp, 1)
            chain(d.tensor_scalar(lg[:, :, 10, 2], lg[:, :, 10, 1], 1.0, None, ALU.add))
            chain(d.reciprocal(lg[:, :, 10, 3], lg[:, :, 10, 2]))
            chain(d.tensor_tensor(lg[:, :, 10, 4], lg[:, :, 10, 3], lg[:, :, 10, 1], ALU.mult))
            for t in range(TT):
                chain(d.tensor_scalar(lg[:, t, 5, :], lg[:, t, 3, :], lg[:, t, 10, 3:4], None, ALU.mult))
                chain(d.scalar_tensor_tensor(out=comb[:, t, 0:NE], in0=lg[:, t, 4, :], scalar=lg[:, t, 10, 4:5],
                                             in1=lg[:, t, 5, :], op0=ALU.mult, op1=ALU.add))
            chain(d.tensor_copy(comb[:, :, NE:2 * NE], comb[:, :, 0:NE]))
            d.wait_ge(count_done, 3)
            d.wait_ge(mask_ready, 1)
            for t in range(TT):
                chain(d.scalar_tensor_tensor(out=lg[:, t, 6, :], in0=bank[6 + t][:, 0:NE], scalar=1.0,
                                             in1=lg[:, t, 8, :], op0=ALU.add, op1=ALU.mult))
            chain(d.tensor_scalar(pos[:, :, 0:NE], lg[:, :, 6, :], -1.0, None, ALU.add))
            chain(d.tensor_scalar(pos[:, :, NE:2 * NE], lg[:, :, 6, :], -1.0 - P, None, ALU.add))

            def dispatch(k):
                for t in range(TT):
                    d.tensor_scalar(disp[:, t, :], iota[:, 0:P], pos[:, t, bass.ds(k, 1)], None,
                                    ALU.is_equal).then_inc(disp_ready, 1)

            def gathered_lo(k):
                for h in range(2):
                    d.wait_ge(ehi_ready, 2 * k + h + 1)
                    d.tensor_tensor(xlo[:, 4 * h:4 * h + 4, 0:P], bank[(7, 1)[h]][:, :].rearrange("p (c t) -> p c t", c=4),
                                    xhi[:, 4 * h:4 * h + 4, 0:P].bitcast(F32), ALU.subtract).then_inc(elo_ready, 1)

            dispatch(0)
            chain(d.tensor_reduce(cnt[:, 0:1], bank[5][:, 0:NE], AX.X, ALU.max))
            chain(d.tensor_scalar(cnt[:, 1:2], cnt[:, 0:1], float(P), None, ALU.is_gt))
            d.tensor_copy(over[:, :], cnt[:, 1:2]).then_inc(over_ready, 1)
            splits_to(2 * MOE + AHEAD)
            gathered_lo(0)
            for free in (added, ehid_ready, ehidT_lo, ylo_ready):
                d.sem_inc(free, 1)

            def expert(i, last):
                mine = [2 * MOE + AHEAD]

                def more(n_):
                    while mine[0] < min(2 * MOE + n_, 2 * (MOE + PER) + (0 if last else AHEAD)):
                        split_lo(d, mine[0], i)
                        mine[0] += 1

                def after(n_):
                    more(n_ + AHEAD)
                    d.wait_ge(half_done, i * (2 * PER) + 2 * MOE + n_)

                for c in range(EB + 1):
                    more(2 * ((moe_gate[c] if c < EB else moe_down[c - 2]) + 2) + AHEAD)
                    if c == 2:
                        d.wait_ge(dispT_done, 1 + i + 1)
                        d.tensor_copy(dispT, bank[7][:, 0:T].rearrange("p (t s) -> p t s", t=TT)).then_inc(dispT_ready, 1)
                        d.tensor_copy(gslot[:, :], bank[7][:, T:T + 1]).then_inc(dispT_ready, 1)
                    if c == 4 and not last:
                        dispatch(i + 1)
                    if c >= 1:
                        d.wait_ge(ehidT_hi, i * EB + c)
                        d.tensor_tensor(hlo[:, (c - 1) % 2, :], bank[6][:, :], hhi[:, (c - 1) % 2, :].bitcast(F32),
                                        ALU.subtract).then_inc(ehidT_lo, 1)
                    if c < EB:
                        after(2 * (moe_up[c] + 2))
                        d.wait_ge(act_ready, i * EB + c + 1)
                        d.wait_ge(ehidT_done, 1 + i * EB + max(c - 1, 0))
                        d.tensor_tensor(ehid[:, c % 2, :], act[:, c % 2, :], bank[2 + c % 2][:, :], ALU.mult).then_inc(ehid_ready, 1)
                if not last:
                    gathered_lo(i + 1)
                after(2 * PER)
                for h in range(2):
                    d.wait_ge(yhi_ready, i * 2 + h + 1)
                    d.scalar_tensor_tensor(out=ylo[:, h, :, :], in0=bank[4 + h][:, :].rearrange("p (c n) -> p c n", c=4),
                                           scalar=gslot[:, 0:1], in1=yhi[:, h, :, :].bitcast(F32), op0=ALU.mult,
                                           op1=ALU.subtract).then_inc(ylo_ready, 1)
                if not last:
                    more(2 * PER + AHEAD)
                for h in range(2):
                    for t in range(TT):
                        d.wait_ge(scattered, i * 4 + 2 * h + t + 1)
                        r_ = resid[:, t, h * 512:(h + 1) * 512]
                        d.tensor_tensor(r_, r_, bank[(1, 3, 6, 7)[2 * h + t]][:, :], ALU.add).then_inc(
                            out_ready if last else added, 1)

            run(d, expert)


def kernel(**inputs):
    import numpy as np
    import concourse.bacc as bacc
    from concourse.bass_utils import run_bass_kernel_spmd

    nc = bacc.Bacc("TRN2", target_bir_lowering=False, num_devices=1,
                   dynamic_dma_scratch_size=1024)
    arrays, args = {}, {}
    for name, value in inputs.items():
        value = np.ascontiguousarray(value)
        arrays[f"in_{name}"] = value
        args[name] = nc.dram_tensor(f"in_{name}", value.shape, mybir.dt.from_np(value.dtype), kind="ExternalInput").ap()
    shape = inputs["x"].shape
    result = nc.dram_tensor("out_x", shape, F32, kind="ExternalOutput").ap()
    build_trunk(nc, args, result)
    ran = run_bass_kernel_spmd(nc, [arrays], core_ids=[0])
    return ran.results[0]["out_x"]
```
